# Optimizing a Trainium2 kernel written in Bass

```python
import math
import jax, jax.numpy as jnp
from jax import lax
import numpy as np

D_MODEL = 1024
BATCH = 1
SEQ = 256
DEPTH = 1

HEAD_DIM = 64
MOBA_HEADS = 8
SB_HEADS = 8
MOBA_WIDTH = MOBA_HEADS * HEAD_DIM
SB_WIDTH = SB_HEADS * HEAD_DIM
MOBA_BLOCK = 256
MOBA_TOPK = 3
MOBA_Q_CHUNK = 16
SB_Q_BLOCK = 128
MEM_TOKENS = 256
X_HEADS = 4
X_HEAD_DIM = 128
X_WIDTH = X_HEADS * X_HEAD_DIM
D_FF = 4 * D_MODEL
IN_COLS = 3 * MOBA_WIDTH + 3 * SB_WIDTH + 2 * D_MODEL
RMS_EPS = 1e-6
NEG = -1e30

kernel_name = "hybrid_moba_stickbreak_gated_block"

def rmsnorm(x, g):
    x32 = x.astype(jnp.float32)
    y = x32 * lax.rsqrt(jnp.mean(x32 * x32, axis=-1, keepdims=True) + RMS_EPS)
    return (y * g.astype(jnp.float32)).astype(x.dtype)

def split_heads(t, n):
    B, S, _ = t.shape
    return t.reshape(B, S, n, -1).transpose(0, 2, 1, 3)

def merge_heads(t):
    B, H, S, dh = t.shape
    return t.transpose(0, 2, 1, 3).reshape(B, S, H * dh)

def alibi_slopes(n_heads):
    return jnp.asarray([2.0 ** (-8.0 * (h + 1) / n_heads) for h in range(n_heads)], dtype=jnp.float32)

def moba_attention(q, k, v):
    B, H, S, dh = q.shape
    scale = dh ** -0.5
    nb = -(-S // MOBA_BLOCK)
    pad = nb * MOBA_BLOCK - S
    kp = jnp.pad(k, ((0, 0), (0, 0), (0, pad), (0, 0)))
    vp = jnp.pad(v, ((0, 0), (0, 0), (0, pad), (0, 0)))
    kb = kp.reshape(B, H, nb, MOBA_BLOCK, dh)
    vb = vp.reshape(B, H, nb, MOBA_BLOCK, dh)
    k_mean = jnp.mean(kb.astype(jnp.float32), axis=3)
    slopes = alibi_slopes(H)
    topk = min(MOBA_TOPK, nb)
    nc = S // MOBA_Q_CHUNK
    q_chunks = q.reshape(B, H, nc, MOBA_Q_CHUNK, dh).transpose(2, 0, 1, 3, 4)
    bi = jnp.arange(B)[:, None, None, None]
    hi = jnp.arange(H)[None, :, None, None]
    blk_ar = jnp.arange(MOBA_BLOCK)

    def chunk(args):
        c, qx = args
        start = c * MOBA_Q_CHUNK
        t = (start + jnp.arange(MOBA_Q_CHUNK)).astype(jnp.int32)
        blk = start // MOBA_BLOCK
        qx32 = qx.astype(jnp.float32)
        gate = jnp.einsum('bhqd,bhnd->bhqn', qx32, k_mean)
        gate = jnp.where(jnp.arange(nb) < blk, gate, NEG)
        _, idx = lax.top_k(gate, topk)
        valid = idx < blk
        k_sel = kb[bi, hi, idx]
        v_sel = vb[bi, hi, idx]
        s_sel = jnp.einsum('bhqd,bhqnkd->bhqnk', qx, k_sel).astype(jnp.float32) * scale
        k_pos = idx[..., None] * MOBA_BLOCK + blk_ar
        dist = (t[None, None, :, None, None] - k_pos).astype(jnp.float32)
        s_sel = s_sel - slopes[None, :, None, None, None] * dist
        s_sel = jnp.where(valid[..., None], s_sel, NEG).reshape(B, H, MOBA_Q_CHUNK, topk * MOBA_BLOCK)
        k_own = lax.dynamic_slice_in_dim(kp, blk * MOBA_BLOCK, MOBA_BLOCK, axis=2)
        v_own = lax.dynamic_slice_in_dim(vp, blk * MOBA_BLOCK, MOBA_BLOCK, axis=2)
        own_pos = blk * MOBA_BLOCK + blk_ar
        d_own = (t[:, None] - own_pos[None, :]).astype(jnp.float32)
        s_own = jnp.einsum('bhqd,bhkd->bhqk', qx, k_own).astype(jnp.float32) * scale
        s_own = s_own - slopes[None, :, None, None] * d_own
        s_own = jnp.where(own_pos[None, :] <= t[:, None], s_own, NEG)
        p = jax.nn.softmax(jnp.concatenate([s_sel, s_own], axis=-1), axis=-1)
        p_sel = p[..., :topk * MOBA_BLOCK].reshape(B, H, MOBA_Q_CHUNK, topk, MOBA_BLOCK).astype(v.dtype)
        p_own = p[..., topk * MOBA_BLOCK:].astype(v.dtype)
        return (jnp.einsum('bhqnk,bhqnkd->bhqd', p_sel, v_sel)
                + jnp.einsum('bhqk,bhkd->bhqd', p_own, v_own))

    out = lax.map(chunk, (jnp.arange(nc, dtype=jnp.int32), q_chunks))
    return out.transpose(1, 2, 0, 3, 4).reshape(B, H, S, dh)

def stick_breaking_attention(q, k, v):
    B, H, S, dh = q.shape
    scale = dh ** -0.5
    outs = []
    for start in range(0, S, SB_Q_BLOCK):
        end = start + SB_Q_BLOCK
        qx = q[:, :, start:end]
        kx = k[:, :, :end]
        vx = v[:, :, :end]
        z = jnp.einsum('bhqd,bhkd->bhqk', qx, kx).astype(jnp.float32) * scale
        t = start + jnp.arange(SB_Q_BLOCK)
        s = jnp.arange(end)
        causal = s[None, :] < t[:, None]
        sp = jnp.where(causal, jax.nn.softplus(z), 0.0)
        log_rest = lax.cumsum(sp, axis=3, reverse=True) - sp
        a = jnp.where(causal, jnp.exp(jax.nn.log_sigmoid(z) - log_rest), 0.0)
        outs.append(jnp.einsum('bhqk,bhkd->bhqd', a.astype(v.dtype), vx))
    return jnp.concatenate(outs, axis=2)

def cross_attention(h, mem_n, w_q, w_kv, w_o):
    q = split_heads(h @ w_q, X_HEADS)
    kv = mem_n @ w_kv
    k = split_heads(kv[..., :X_WIDTH], X_HEADS)
    v = split_heads(kv[..., X_WIDTH:], X_HEADS)
    s = jnp.einsum('bhqd,bhkd->bhqk', q, k).astype(jnp.float32) * (X_HEAD_DIM ** -0.5)
    p = jax.nn.softmax(s, axis=-1).astype(v.dtype)
    return merge_heads(jnp.einsum('bhqk,bhkd->bhqd', p, v)) @ w_o

def setup_inputs(seed: int = 0) -> dict:
    key = jax.random.key(seed)
    ks = jax.random.split(key, 20)

    def w(k, shape, fan_in):
        return jax.random.normal(k, shape, jnp.float32) * (fan_in ** -0.5)

    def gain(k, shape):
        return 1.0 + 0.02 * jax.random.normal(k, shape, jnp.float32)

    L = DEPTH
    return {
        "x": jax.random.normal(ks[0], (BATCH, SEQ, D_MODEL), jnp.float32),
        "mem": jax.random.normal(ks[1], (BATCH, MEM_TOKENS, D_MODEL), jnp.float32),
        "g_mix": gain(ks[2], (L, D_MODEL)),
        "w_in": w(ks[3], (L, D_MODEL, IN_COLS), D_MODEL),
        "w_br_moba": w(ks[4], (L, MOBA_WIDTH, D_MODEL), MOBA_WIDTH),
        "w_br_sb": w(ks[5], (L, SB_WIDTH, D_MODEL), SB_WIDTH),
        "w_out": w(ks[6], (L, D_MODEL, D_MODEL), D_MODEL),
        "g_cross": gain(ks[7], (L, D_MODEL)),
        "g_mem": gain(ks[8], (L, D_MODEL)),
        "w_xq": w(ks[9], (L, D_MODEL, X_WIDTH), D_MODEL),
        "w_xkv": w(ks[10], (L, D_MODEL, 2 * X_WIDTH), D_MODEL),
        "w_xo": w(ks[11], (L, X_WIDTH, D_MODEL), X_WIDTH),
        "g_mlp": gain(ks[12], (L, D_MODEL)),
        "w_up": w(ks[13], (L, D_MODEL, D_FF), D_MODEL),
        "w_down": w(ks[14], (L, D_FF, D_MODEL), D_FF),
        "g_final": gain(ks[15], (D_MODEL,)),
    }

def reference(x, mem, g_mix, w_in, w_br_moba, w_br_sb, w_out, g_cross, g_mem,
              w_xq, w_xkv, w_xo, g_mlp, w_up, w_down, g_final):
    o1 = 3 * MOBA_WIDTH
    o2 = o1 + 3 * SB_WIDTH
    o3 = o2 + D_MODEL
    for l in range(DEPTH):
        h = rmsnorm(x, g_mix[l])
        proj = h @ w_in[l]
        qa = split_heads(proj[..., 0:MOBA_WIDTH], MOBA_HEADS)
        ka = split_heads(proj[..., MOBA_WIDTH:2 * MOBA_WIDTH], MOBA_HEADS)
        va = split_heads(proj[..., 2 * MOBA_WIDTH:o1], MOBA_HEADS)
        qb = split_heads(proj[..., o1:o1 + SB_WIDTH], SB_HEADS)
        kbh = split_heads(proj[..., o1 + SB_WIDTH:o1 + 2 * SB_WIDTH], SB_HEADS)
        vbh = split_heads(proj[..., o1 + 2 * SB_WIDTH:o2], SB_HEADS)
        gate_a = jax.nn.sigmoid(proj[..., o2:o3])
        gate_b = jax.nn.sigmoid(proj[..., o3:])
        y_a = merge_heads(moba_attention(qa, ka, va)) @ w_br_moba[l]
        y_b = merge_heads(stick_breaking_attention(qb, kbh, vbh)) @ w_br_sb[l]
        x = x + (gate_a * y_a + gate_b * y_b) @ w_out[l]
        x = x + cross_attention(rmsnorm(x, g_cross[l]), rmsnorm(mem, g_mem[l]),
                                w_xq[l], w_xkv[l], w_xo[l])
        u = rmsnorm(x, g_mlp[l]) @ w_up[l]
        x = x + jnp.square(jax.nn.relu(u)) @ w_down[l]
    return rmsnorm(x, g_final)


_drawn_inputs = setup_inputs


def setup_inputs(seed=0):
    import zlib

    import numpy as np

    out = dict(_drawn_inputs(seed))
    spreads = {}
    factors = {'g_mix': 5.273, 'g_cross': 8.0, 'g_mem': 8.0, 'g_mlp': 9.989, 'g_final': 8.056}
    for name, (base, spread) in spreads.items():
        noise = np.random.default_rng([zlib.crc32(name.encode()), seed]).standard_normal(out[name].shape)
        drawn = base * np.exp(spread * noise) if base else spread * noise
        out[name] = __import__('jax').numpy.asarray(drawn.astype(out[name].dtype))
    for name, factor in factors.items():
        out[name] = (out[name] * factor).astype(out[name].dtype)
    return out
```

```python
import concourse.bass as bass
from concourse import mybir
from contextlib import ExitStack

P = 128


def hybrid_layer(nc, x, mem, g_mix, w_in, w_br_moba, w_br_sb, w_out, g_cross, g_mem,
                 w_xq, w_xkv, w_xo, g_mlp, w_up, w_down, g_final, out):
    fp32, f32r = mybir.dt.float32, mybir.dt.float32r
    ACT, ALU = mybir.ActivationFunctionType, mybir.AluOpType
    AX = mybir.AxisListType.X

    SEQ, D = x.shape[1], x.shape[2]
    TOK = SEQ // P
    KT = D // P
    HEADS, DH = 8, 64
    WIDTH = HEADS * DH
    XH, XDH = 4, 128
    XW = XH * XDH
    FF = w_up.shape[2]
    RING, RAW = 4, 2
    CH = 2048
    PAIRS = FF // (2 * P)
    EPS, NEG = 1e-6, -1e30
    assert (SEQ, TOK, KT) == (256, 2, 8)

    def by_cols(w, k0, nk, c0, nc_):
        return w[0, k0 * P:(k0 + nk) * P, c0:c0 + nc_].rearrange("(k p) n -> p k n", p=P)

    QKV = 3 * WIDTH
    stream = []
    for base in (0, QKV):
        stream += [by_cols(w_in, 0, 8, base + 256 * j, 256) for j in range(4)]
    for base in (2 * WIDTH, QKV + 2 * WIDTH):
        stream += [by_cols(w_in, 4 * j, 4, base, 512) for j in range(2)]
    GATE0 = len(stream)
    stream += [by_cols(w_in, 0, 8, 2 * QKV + 256 * j, 256) for j in range(8)]
    mem_k = [by_cols(w_xkv, 0, 8, 256 * j, 256) for j in range(2)]
    mem_v = [by_cols(w_xkv, 4 * j, 4, XW, 512) for j in range(2)]
    MK = [len(stream)]
    stream.append(mem_k[0])
    BR0 = len(stream)
    for n in range(2):
        stream += [by_cols(w, 0, 4, 512 * n, 512) for w in (w_br_moba, w_br_sb)]
    OUT0 = len(stream)
    stream += [by_cols(w_out, 2 * j, 2, 0, 1024) for j in range(4)]
    MK.append(len(stream))
    MV = [len(stream) + 1, len(stream) + 4]
    XQ0 = len(stream) + 2
    stream += [mem_k[1], mem_v[0]] + [by_cols(w_xq, 0, 8, 256 * j, 256) for j in range(2)] + [mem_v[1]]
    XO0 = len(stream)
    stream += [by_cols(w_xo, 2 * j, 2, 0, 1024) for j in range(2)]
    UP0 = len(stream)
    stream += [by_cols(w_up, 0, 8, 0, 256), by_cols(w_up, 0, 8, 256, 256), by_cols(w_down, 0, 2, 0, 1024)]
    LOOP0 = len(stream)
    ITERS = (PAIRS - 2) // 2
    LAST = LOOP0 + 4 * ITERS
    assert LOOP0 == 39 and LAST == 67 and PAIRS == 2 * ITERS + 2

    def up_cols(i):
        return w_up[0, :, bass.ds(i * 256, 256)].rearrange("(k p) n -> p k n", p=P)

    def down_rows(i):
        return w_down[0, bass.ds(i * 256, 256), :].rearrange("(k p) n -> p k n", p=P)

    ctx = ExitStack()
    with ctx:
        at = [(nc.sbuf_base + 31) // 32 * 32]

        def place(name, shape, dt=fp32, over=None):
            size = 4
            for s in shape[1:]:
                size *= s
            offset = at[0] if over is None else over
            t = nc.alloc_sbuf_tensor_at(name, shape, dt, offset=offset)
            if over is None:
                at[0] += (size + 31) // 32 * 32
            return t, offset

        def sb(name, shape, dt=fp32, over=None):
            return place(name, shape, dt, over)[0]

        def sem(name):
            return ctx.enter_context(nc.semaphore(name))

        raw = sb("raw", [P, RAW, CH])
        w_hi = sb("w_hi", [P, RING, CH], f32r)
        w_lo = sb("w_lo", [P, RING, CH], f32r)
        res = sb("res", [P, TOK, D])
        hT_hi = sb("hT_hi", [P, KT, SEQ], f32r)
        hT_lo = sb("hT_lo", [P, KT, SEQ], f32r)
        mT_hi = sb("mT_hi", [P, KT, SEQ], f32r)
        mT_lo = sb("mT_lo", [P, KT, SEQ], f32r)
        qkT, o = place("qkT", [P, 16, SEQ])
        mixT_hi = sb("mixT_hi", [P, KT, SEQ], f32r, over=o)
        mixT_lo = sb("mixT_lo", [P, KT, SEQ], f32r, over=o + 8192)
        xqT = sb("xqT", [P, XH, SEQ], over=o)
        v_tok, o = place("v_tok", [P, TOK, 2 * WIDTH])
        mkT = sb("mkT", [P, XH, SEQ], over=o)
        mv_tok = sb("mv_tok", [P, TOK, XW], over=o + 4096)
        gfin = sb("gfin", [P, D], over=o)
        gateT, o = place("gateT", [P, 16, SEQ])
        xs = sb("xs", [P, TOK, D], over=o)
        mem_tok = sb("mem_tok", [P, TOK, D], over=o + 8192)
        aT_hi = sb("aT_hi", [P, 8, SEQ], f32r)
        aT_lo = sb("aT_lo", [P, 8, SEQ], f32r)
        alibi, o = place("alibi", [P, HEADS, SEQ])
        mo_u = sb("mo_u", [P, 2, 384])
        mo_pT = sb("mo_pT", [P, 2, 384])
        sb_aT = sb("sb_aT", [P, 2, 384])
        sb_t = sb("sb_t", [P, 384])
        sb_sp = sb("sb_sp", [P, 2, 384])
        gated_a = sb("gated_a", [P, 2, 512], over=o)
        gated_b = sb("gated_b", [P, 2, 512], over=o + 4096)
        x_p = sb("x_p", [P, XH, 512], over=o)
        x_pT = sb("x_pT", [P, XH, 512], over=o + 8192)
        relu = sb("relu", [P, 2, 512], over=o)
        relu2 = sb("relu2", [P, 2, 512], over=o + 4096)
        ident = sb("ident", [P, P])
        neg_tri = sb("neg_tri", [P, P])
        neg_ones = sb("neg_ones", [P, P])
        ident_r = sb("ident_r", [P, P], f32r)
        future_r = sb("future_r", [P, 2, P], f32r)
        g_rows = sb("g_rows", [32, P])
        gT = sb("gT", [P, 32])
        half = sb("half", [P, 2])
        stat = sb("stat", [P, 5, 2])
        var = sb("var", [P, 5, 2])
        rstd = sb("rstd", [P, 5, 2])
        mo_max = sb("mo_max", [P, 2])
        mo_nmax = sb("mo_nmax", [P, 2])
        mo_sum = sb("mo_sum", [P, 2])
        mo_rsum = sb("mo_rsum", [P, 2])
        x_scale = sb("x_scale", [P, 2])
        x_max = sb("x_max", [P, XH, 2])
        x_bias = sb("x_bias", [P, XH, 2])
        x_sum = sb("x_sum", [P, XH, 2])
        x_rsum = sb("x_rsum", [P, XH, 2])
        assert at[0] <= nc.sbuf_usable_end
        X, MEM, X1, X2, X3 = range(5)
        G_MIX, G_CROSS, G_MEM, G_MLP = range(0, 32, 8)

        bank = [ctx.enter_context(nc.psum_tensor(f"bank{i}", [P, 512], fp32))[:, :] for i in range(8)]
        MO_S, MO_PT, SB_Z, MO_O, SB_O = 2, 3, (4, 5), 6, 7

        x_in = [sem(f"x_in{t}") for t in range(TOK)]
        g_in, mem_in, gfin_in = sem("g_in"), sem("mem_in"), sem("gfin_in")
        raw_in = [sem(f"raw_in{s}") for s in range(RAW)]
        stored = sem("stored")
        ident_ready, masks_ready, alibi_ready = sem("ident_ready"), sem("masks_ready"), sem("alibi_ready")
        pool_step, dve_step = sem("pool_step"), sem("dve_step")
        w_hi_ready, w_lo_ready, w_used = sem("w_hi_ready"), sem("w_lo_ready"), sem("w_used")
        half_ready, sumsq_act, sumsq_dve = sem("half_ready"), sem("sumsq_act"), sem("sumsq_dve")
        rstd_ready = sem("rstd_ready")
        xs_act, xs_dve, mem_scaled = sem("xs_act"), sem("xs_dve"), sem("mem_scaled")
        gT_done, gT_ready = sem("gT_done"), sem("gT_ready")
        NAMES = {X: "x", MEM: "mem", X1: "x1", X2: "x2"}
        transposed = {n: sem(f"{s}_transposed") for n, s in NAMES.items()}
        hi_done = {n: sem(f"{s}_hi_done") for n, s in NAMES.items()}
        lo_done = {n: sem(f"{s}_lo_done") for n, s in NAMES.items()}
        qk_evac, v_evac, gate_evac = sem("qk_evac"), sem("v_evac"), sem("gate_evac")
        mo_s, mo_biased, mo_exp, mo_normed = sem("mo_s"), sem("mo_biased"), sem("mo_exp"), sem("mo_normed")
        mo_t, mo_pt, mo_av = sem("mo_t"), sem("mo_pt"), sem("mo_av")
        sb_z, sb_abs, sb_e, sb_ln = sem("sb_z"), sem("sb_abs"), sem("sb_e"), sem("sb_ln")
        sb_raw, sb_c = sem("sb_raw"), sem("sb_c")
        sb_exp, sb_av = sem("sb_exp"), sem("sb_av")
        att_hi, att_lo = sem("att_hi"), sem("att_lo")
        sig_ready = sem("sig_ready")
        mixed, mix_hi, mix_lo = sem("mixed"), sem("mix_hi"), sem("mix_lo")
        x1_ready, x2_ready = sem("x1_ready"), sem("x2_ready")
        mk_evac, mv_evac, xq_evac = sem("mk_evac"), sem("mv_evac"), sem("xq_evac")
        x_s, x_biased, x_exp, x_normed = sem("x_s"), sem("x_biased"), sem("x_exp"), sem("x_normed")
        x_t, x_pt, x_av, xo_hi, xo_lo = sem("x_t"), sem("x_pt"), sem("x_av"), sem("xo_hi"), sem("xo_lo")
        u_relu, u_sq, u_hi, u_lo = sem("u_relu"), sem("u_sq"), sem("u_hi"), sem("u_lo")
        tile_done, x3_ready, fin = sem("tile_done"), sem("x3_ready"), sem("fin")

        block = ctx.enter_context(nc.Block())

        @block.sync
        def _(sp):
            def load(c, src, slot, used=None):
                if used is not None:
                    sp.wait_ge(w_lo_ready, used)
                sp.dma_start(raw[:, slot, :].rearrange("p (k n) -> p k n", k=src.shape[1]), src)\
                    .then_inc(raw_in[slot], 16)

            for t in range(TOK):
                sp.dma_start(res[:, t, :], x[0, t * P:(t + 1) * P, :]).then_inc(x_in[t], 16)
            for c in range(RAW):
                load(c, stream[c], c)
            sp.dma_start(mem_tok[:, :, :], mem[0, :, :].rearrange("(t p) d -> p t d", p=P)).then_inc(mem_in, 16)
            for c in range(RAW, LOOP0):
                load(c, stream[c], c % RAW, c - RAW + 1)
            with sp.Fori(0, ITERS) as i:
                for j in range(4):
                    src = (up_cols if j % 2 == 0 else down_rows)(2 * i + (2 + j // 2 if j % 2 == 0 else 1 + j // 2))
                    load(None, src, (LOOP0 + j) % RAW, 4 * i + (LOOP0 + j - RAW + 1))
            load(LAST, by_cols(w_down, 2 * (PAIRS - 1), 2, 0, 1024), LAST % RAW, LAST - RAW + 1)
            sp.wait_ge(x_av, XH)
            sp.dma_start(gfin[:, :], g_final.rearrange("(a d) -> a d", a=1).to_broadcast([P, D])).then_inc(gfin_in, 16)
            for t in range(TOK):
                sp.wait_ge(fin, t + 1)
                sp.dma_start(out[0, t * P:(t + 1) * P, :], xs[:, t, :]).then_inc(stored, 16)
            sp.wait_ge(stored, 16 * TOK)

        @block.gpsimd
        def _(pool):
            steps = [0]

            def step(ins):
                steps[0] += 1
                ins.then_inc(pool_step, 1)
                pool.wait_ge(pool_step, steps[0])

            nc.gpsimd.memset(half[:, :], -0.5).then_inc(half_ready, 1)
            step(nc.gpsimd.memset(ident[:, :], 0.0))
            nc.gpsimd.affine_select(out=ident[:, :], in_=ident[:, :], compare_op=ALU.not_equal, fill=1.0, base=0,
                                    pattern=[[-1, P]], channel_multiplier=1).then_inc(ident_ready, 1)

            def rsqrt(n, t0=0, t1=TOK):
                step(nc.gpsimd.tensor_scalar(var[:, n, t0:t1], stat[:, n, t0:t1], 1.0 / D, EPS, ALU.mult, ALU.add))
                nc.gpsimd.tensor_tensor(rstd[:, n, t0:t1], var[:, n, t0:t1], half[:, t0:t1], ALU.pow)\
                    .then_inc(rstd_ready, 1)

            pool.wait_ge(half_ready, 1)
            pool.wait_ge(sumsq_act, 1)
            pool.wait_ge(sumsq_dve, 1)
            rsqrt(X)
            step(nc.gpsimd.memset(neg_ones[:, :], -1.0))
            nc.gpsimd.affine_select(out=neg_tri[:, :], in_=neg_ones[:, :], compare_op=ALU.is_ge, fill=0.0, base=0,
                                    pattern=[[-1, P]], channel_multiplier=1).then_inc(masks_ready, 1)
            step(nc.gpsimd.memset(future_r[:, :, :].bitcast(fp32), 0.0))
            step(nc.gpsimd.affine_select(out=future_r[:, :, :], in_=future_r[:, :, :].bitcast(fp32),
                                         compare_op=ALU.is_gt, fill=NEG, base=0, pattern=[[0, 2], [1, P]],
                                         channel_multiplier=-1))
            nc.gpsimd.tensor_copy(ident_r[:, :], ident[:, :]).then_inc(masks_ready, 1)
            step(nc.gpsimd.iota(alibi[:, 0, :], pattern=[[1, SEQ]], base=-P, channel_multiplier=-1,
                                allow_small_or_imprecise_dtypes=True))
            for h in range(HEADS - 1, -1, -1):
                step(nc.gpsimd.tensor_scalar(alibi[:, h, :], alibi[:, 0, :], 2.0 ** (-8.0 * (h + 1) / HEADS), 0.0,
                                             ALU.mult, ALU.add))
            for h in range(HEADS):
                last = nc.gpsimd.affine_select(out=alibi[:, h, :], in_=alibi[:, h, :], compare_op=ALU.is_ge, fill=NEG,
                                               base=P, pattern=[[-1, SEQ]], channel_multiplier=1)
                last.then_inc(alibi_ready, 1)
            pool.wait_ge(sumsq_dve, 2)
            rsqrt(MEM)

            pool.wait_ge(sumsq_dve, 3)
            rsqrt(X1)
            pool.wait_ge(sumsq_act, 2)
            rsqrt(X3, 0, 1)
            pool.wait_ge(sumsq_dve, 4)
            rsqrt(X3, 1, 2)

        T_BANKS = {X: (range(8), 1), MEM: ((4, 5, 6, 7), 2), X1: ((0, 1, 2, 3), 2), X2: ((0, 1, 7, 4), 2)}

        def t_tile(n, k):
            banks, per = T_BANKS[n]
            return bank[banks[k // per]][:, SEQ * (k % per):SEQ * (k % per) + SEQ]

        def bank_full(n, k):
            per = T_BANKS[n][1]
            return (k // per + 1) * per

        def flat(t):
            return t.rearrange("p b t -> p (b t)")

        @block.scalar
        def _(act):
            copy = nc.scalar.activation

            for j, g in enumerate((g_mix, g_cross, g_mem, g_mlp)):
                act.dma_start(g_rows[8 * j:8 * j + 8, :], g[0, :].rearrange("(k p) -> k p", p=P)).then_inc(g_in, 16)

            def split_hi(slot, rslot, arrived, used=None):
                act.wait_ge(raw_in[rslot], arrived)
                if used is not None:
                    act.wait_ge(w_used, used)
                copy(w_hi[:, slot, :], raw[:, rslot, :], ACT.Copy).then_inc(w_hi_ready, 1)

            def split(c):
                split_hi(c % RING, c % RAW, 16 * (c // RAW + 1), c - RING + 1 if c >= RING else None)

            def high_T(n, k, dst, g):
                act.wait_ge(transposed[n], bank_full(n, k))
                copy(dst[:, k, :], t_tile(n, k), ACT.Copy, scale=gT[:, g + k:g + k + 1]).then_inc(hi_done[n], 1)

            act.wait_ge(x_in[0], 16)
            copy(xs[:, 0, :], res[:, 0, :], ACT.Square, accum_out=stat[:, X, 0:1]).then_inc(sumsq_act, 1)
            act.wait_ge(rstd_ready, 1)
            copy(xs[:, 0, :], res[:, 0, :], ACT.Copy, scale=rstd[:, X, 0:1]).then_inc(xs_act, 1)
            act.wait_ge(gT_ready, 1)
            for k in range(KT):
                high_T(X, k, hT_hi, G_MIX)
                if k == 3:
                    split(0)
            for c in range(1, RING):
                split(c)
            with act.Fori(0, 2) as i:
                for j in range(4):
                    act.wait_ge(w_used, 4 * i + (j + 1))
                    copy(flat(qkT[:, bass.ds(8 * i + 2 * j, 2), :]), bank[j][:, :], ACT.Copy,
                         scale=DH ** -0.5 if j < 2 else 1.0).then_inc(qk_evac, 1)
                    split_hi(j, j % 2, 32 * i + 16 * (j // 2 + 3))
            for k in range(KT):
                high_T(MEM, k, mT_hi, G_MEM)
                if k == 3:
                    split(12)
            for b in range(2):
                act.wait_ge(w_used, 10 + 2 * b)
                for t in range(TOK):
                    copy(v_tok[:, t, b * WIDTH:(b + 1) * WIDTH], bank[2 * b + t][:, :], ACT.Copy).then_inc(v_evac, 1)
                split(13 + b)

            def evac_gate(g):
                act.wait_ge(w_used, GATE0 + g + 1)
                copy(flat(gateT[:, 2 * g:2 * g + 2, :]), bank[g % 2][:, :], ACT.Copy).then_inc(gate_evac, 1)

            def att_high(p):
                act.wait_ge(mo_av, 2 * p + 2)
                copy(aT_hi[:, p, :], bank[MO_O][:, 0:SEQ], ACT.Copy).then_inc(att_hi, 1)
                act.wait_ge(sb_av, 2 * p + 2)
                copy(aT_hi[:, 4 + p, :], bank[SB_O][:, 0:SEQ], ACT.Copy).then_inc(att_hi, 1)

            for h in range(HEADS):
                z = bank[SB_Z[h % 2]][:, 0:384]
                act.wait_ge(sb_z, h + 1)
                if h:
                    act.wait_ge(sb_raw, h)
                copy(sb_t[:, :], z, ACT.Abs).then_inc(sb_abs, 1)
                act.wait_ge(sb_abs, h + 1)
                copy(sb_t[:, :], sb_t[:, :], ACT.Exp, scale=-1.0).then_inc(sb_e, 1)
                act.wait_ge(sb_e, h + 1)
                copy(sb_t[:, :], sb_t[:, :], ACT.Ln, bias=1.0).then_inc(sb_ln, 1)
                act.wait_ge(mo_biased, h + 1)
                for q, (a, b) in enumerate(((0, 128), (128, 384))):
                    last = copy(mo_u[:, h % 2, a:b], mo_u[:, h % 2, a:b], ACT.Exp, bias=mo_nmax[:, q:q + 1],
                                accum_out=mo_sum[:, q:q + 1])
                last.then_inc(mo_exp, 1)
                if h:
                    evac_gate(h - 1)
                split(GATE0 + h + 3)
                if h >= 2 and h % 2 == 0:
                    att_high(h // 2 - 1)
                act.wait_ge(sb_c, h + 1)
                if h >= 2:
                    act.wait_ge(sb_av, h - 1)
                copy(sb_aT[:, h % 2, :], z, ACT.Exp).then_inc(sb_exp, 1)
            evac_gate(7)
            att_high(3)
            split(23)
            act.wait_ge(w_used, MK[0] + 1)
            copy(flat(mkT[:, 0:2, :]), bank[0][:, :], ACT.Copy).then_inc(mk_evac, 1)
            act.wait_ge(gate_evac, 8)
            for n in range(2):
                for b in range(2):
                    s = gateT[:, 8 * b + 4 * n:8 * b + 4 * n + 4, :]
                    copy(s, s, ACT.Sigmoid).then_inc(sig_ready, 1)
                if n == 0:
                    split(24)
            for j in range(4):
                act.wait_ge(mixed, j + 1)
                copy(flat(mixT_hi[:, 2 * j:2 * j + 2, :]), gated_a[:, j % 2, :], ACT.Copy).then_inc(mix_hi, 1)
                if j == 1:
                    split(25)
                    split(26)
            for c in range(27, 32):
                split(c)
            act.wait_ge(w_used, MK[1] + 1)
            copy(flat(mkT[:, 2:4, :]), bank[4][:, :], ACT.Copy).then_inc(mk_evac, 1)
            split(32)
            for k in range(KT):
                high_T(X1, k, hT_hi, G_CROSS)
            split(33)
            for j in range(2):
                act.wait_ge(w_used, XQ0 + j + 1)
                copy(flat(xqT[:, 2 * j:2 * j + 2, :]), bank[(7, 4)[j]][:, :], ACT.Copy).then_inc(xq_evac, 1)
                if j == 0:
                    split(34)
            for h in range(XH):
                act.wait_ge(x_biased, h + 1)
                for t in range(TOK):
                    last = copy(x_p[:, h, SEQ * t:SEQ * t + SEQ], bank[h][:, SEQ * t:SEQ * t + SEQ], ACT.Exp,
                                bias=x_bias[:, h, t:t + 1], scale=x_scale[:, t:t + 1],
                                accum_out=x_sum[:, h, t:t + 1])
                last.then_inc(x_exp, 1)
                if h == 1:
                    split(35)
            act.wait_ge(w_used, MV[1] + 1)
            for t in range(TOK):
                copy(mv_tok[:, t, :], bank[5 + t][:, :], ACT.Copy).then_inc(mv_evac, 1)
            split(36)
            for p in range(2):
                act.wait_ge(x_av, 2 * p + 2)
                copy(flat(aT_hi[:, 2 * p:2 * p + 2, :]), bank[p][:, :], ACT.Copy).then_inc(xo_hi, 1)
            split(37)
            split(38)
            for k in range(KT):
                high_T(X2, k, hT_hi, G_MLP)
            split(39)

            def square_relu(b, used, relu_free, mine):
                act.wait_ge(w_used, used)
                if relu_free is not None:
                    act.wait_ge(u_sq, relu_free)
                copy(relu[:, b, :], bank[b][:, :], ACT.Relu).then_inc(u_relu, 1)
                act.wait_ge(u_relu, mine)
                copy(flat(aT_hi[:, 4 + 2 * b:6 + 2 * b, :]), relu[:, b, :], ACT.Square).then_inc(u_hi, 1)

            square_relu(0, UP0 + 1, None, 1)
            square_relu(1, UP0 + 2, None, 2)
            with act.Fori(0, ITERS) as i:
                for j in range(2):
                    for s in (2 * j + 1, 2 * j + 2):
                        c = LOOP0 + s
                        split_hi(c % RING, c % RAW, 32 * i + 16 * (c // RAW + 1), 4 * i + (c - RING + 1))
                    square_relu(j, 4 * i + (LOOP0 + 2 * j + 1), 2 * i + (j + 1), 2 * i + (j + 3))
            act.wait_ge(x3_ready, 1)
            copy(xs[:, 0, :], res[:, 0, :], ACT.Square, accum_out=stat[:, X3, 0:1]).then_inc(sumsq_act, 1)

        @block.vector
        def _(dve):
            steps = [0]

            def step(ins):
                steps[0] += 1
                ins.then_inc(dve_step, 1)
                dve.wait_ge(dve_step, steps[0])

            sub = ALU.subtract

            def low(dst, whole, high):
                return nc.vector.tensor_tensor(dst, whole, high.bitcast(fp32), sub)

            def split_lo(slot, rslot, hi):
                dve.wait_ge(w_hi_ready, hi)
                low(w_lo[:, slot, :], raw[:, rslot, :], w_hi[:, slot, :]).then_inc(w_lo_ready, 1)

            def split(c):
                split_lo(c % RING, c % RAW, c + 1)

            def low_T(n, k, hi, lo, g):
                dve.wait_ge(hi_done[n], bank_full(n, k))
                nc.vector.scalar_tensor_tensor(lo[:, k, :], t_tile(n, k), gT[:, g + k:g + k + 1],
                                               hi[:, k, :].bitcast(fp32), ALU.mult, sub).then_inc(lo_done[n], 1)

            def sum_squares(scratch, src, n, t):
                return nc.vector.tensor_tensor_reduce(out=scratch, in0=src, in1=src, scale=1.0, scalar=0.0,
                                                      op0=ALU.mult, op1=ALU.add, accum_out=stat[:, n, t:t + 1])

            dve.wait_ge(x_in[1], 16)
            sum_squares(xs[:, 1, :], res[:, 1, :], X, 1).then_inc(sumsq_dve, 1)
            dve.wait_ge(gT_done, 1)
            nc.vector.tensor_copy(gT[:, :], bank[7][:, 256:288]).then_inc(gT_ready, 1)
            dve.wait_ge(rstd_ready, 1)
            nc.vector.tensor_scalar(xs[:, 1, :], res[:, 1, :], rstd[:, X, 1:2], None, ALU.mult).then_inc(xs_dve, 1)
            for k in range(KT):
                low_T(X, k, hT_hi, hT_lo, G_MIX)
                if k == 3:
                    split(0)
            for c in range(1, RING):
                split(c)
            dve.wait_ge(mem_in, 16)
            for t in range(TOK):
                last = sum_squares(xs[:, t, :], mem_tok[:, t, :], MEM, t)
            last.then_inc(sumsq_dve, 1)
            with dve.Fori(0, 2) as i:
                for j in range(4):
                    split_lo(j, j % 2, 4 * i + (j + 5))
            dve.wait_ge(rstd_ready, 2)
            for t in range(TOK):
                nc.vector.tensor_scalar(mem_tok[:, t, :], mem_tok[:, t, :], rstd[:, MEM, t:t + 1], None, ALU.mult)\
                    .then_inc(mem_scaled, 1)
            for k in range(KT):
                low_T(MEM, k, mT_hi, mT_lo, G_MEM)
                if k == 3:
                    split(12)
            split(13)
            split(14)

            def att_low(p):
                for b, o in enumerate((MO_O, SB_O)):
                    dve.wait_ge(att_hi, 2 * p + b + 1)
                    low(aT_lo[:, 4 * b + p, :], bank[o][:, 0:SEQ], aT_hi[:, 4 * b + p, :]).then_inc(att_lo, 1)

            dve.wait_ge(alibi_ready, HEADS)
            for h in range(HEADS):
                dve.wait_ge(mo_s, h + 1)
                if h >= 2:
                    dve.wait_ge(mo_t, h - 1)
                for q, (a, b, c) in enumerate(((0, 128, 128), (128, 384, 0))):
                    last = nc.vector.tensor_tensor_reduce(out=mo_u[:, h % 2, a:b], in0=bank[MO_S][:, a:b],
                                                          in1=alibi[:, h, c:SEQ], scale=1.0, scalar=-3e38,
                                                          op0=ALU.add, op1=ALU.max, accum_out=mo_max[:, q:q + 1])
                step(last)
                nc.vector.tensor_scalar(mo_nmax[:, :], mo_max[:, :], -1.0, None, ALU.mult).then_inc(mo_biased, 1)
                dve.wait_ge(mo_exp, h + 1)
                step(nc.vector.reciprocal(mo_rsum[:, :], mo_sum[:, :]))
                for q, (a, b) in enumerate(((0, 128), (128, 384))):
                    last = nc.vector.tensor_scalar(mo_u[:, h % 2, a:b], mo_u[:, h % 2, a:b], mo_rsum[:, q:q + 1], None,
                                                   ALU.mult)
                last.then_inc(mo_normed, 1)
                dve.wait_ge(sb_ln, h + 1)
                if h >= 2:
                    dve.wait_ge(sb_c, h - 1)
                nc.vector.scalar_tensor_tensor(sb_sp[:, h % 2, :], bank[SB_Z[h % 2]][:, 0:384], 0.0, sb_t[:, :],
                                               ALU.max, ALU.add).then_inc(sb_raw, 1)
                dve.wait_ge(mo_t, h + 1)
                if h >= 2:
                    dve.wait_ge(mo_av, h - 1)
                nc.vector.tensor_copy(mo_pT[:, h % 2, :], bank[MO_PT][:, 0:384]).then_inc(mo_pt, 1)
                split(GATE0 + h + 3)
                if h >= 2 and h % 2 == 0:
                    att_low(h // 2 - 1)
            att_low(3)
            split(23)
            split(24)
            for j in range(4):
                n, jj = j // 2, j % 2
                dve.wait_ge(w_used, BR0 + 2 * n + 1)
                dve.wait_ge(sig_ready, 2 * n + 1)
                if j >= 2:
                    dve.wait_ge(mix_hi, j - 1)
                nc.vector.tensor_tensor(gated_a[:, jj, :], bank[4 * n + jj][:, :], flat(gateT[:, 2 * j:2 * j + 2, :]),
                                        ALU.mult)
                dve.wait_ge(w_used, BR0 + 2 * n + 2)
                dve.wait_ge(sig_ready, 2 * n + 2)
                step(nc.vector.tensor_tensor(gated_b[:, jj, :], bank[4 * n + 2 + jj][:, :],
                                             flat(gateT[:, 8 + 2 * j:10 + 2 * j, :]), ALU.mult))
                nc.vector.tensor_tensor(gated_a[:, jj, :], gated_a[:, jj, :], gated_b[:, jj, :], ALU.add)\
                    .then_inc(mixed, 1)
                dve.wait_ge(mix_hi, j + 1)
                low(flat(mixT_lo[:, 2 * j:2 * j + 2, :]), gated_a[:, jj, :], flat(mixT_hi[:, 2 * j:2 * j + 2, :]))\
                    .then_inc(mix_lo, 1)
                if j == 1:
                    split(25)
                    split(26)
            for c in range(27, 32):
                split(c)

            def wait_tile(t, n, used):
                dve.wait_ge(*((tile_done, n + 1) if t == 0 else (w_used, used)))

            def add_residual(n, used, banks, done):
                for t in range(TOK):
                    wait_tile(t, n, used)
                    for c in range(2):
                        s = res[:, t, 512 * c:512 * c + 512]
                        last = nc.vector.tensor_tensor(s, bank[banks[2 * t + c]][:, :], s, ALU.add)
                    last.then_inc(done, 1)

            add_residual(0, OUT0 + 4, (0, 1, 2, 3), x1_ready)
            dve.wait_ge(x1_ready, TOK)
            for t in range(TOK):
                last = sum_squares(xs[:, t, :], res[:, t, :], X1, t)
            last.then_inc(sumsq_dve, 1)
            split(32)
            for k in range(KT):
                low_T(X1, k, hT_hi, hT_lo, G_CROSS)
            split(33)
            dve.wait_ge(rstd_ready, 3)
            step(nc.vector.tensor_scalar(x_scale[:, :], rstd[:, X1, :], XDH ** -0.5, None, ALU.mult))
            for h in range(XH):
                dve.wait_ge(x_s, h + 1)
                step(nc.vector.tensor_reduce(x_max[:, h, :], bank[h][:, :].rearrange("p (t k) -> p t k", t=TOK),
                                             axis=AX, op=ALU.max))
                nc.vector.scalar_tensor_tensor(x_bias[:, h, :], x_max[:, h, :], -1.0, x_scale[:, :], ALU.mult,
                                               ALU.mult).then_inc(x_biased, 1)
            split(34)
            for h in range(XH):
                dve.wait_ge(x_exp, h + 1)
                step(nc.vector.reciprocal(x_rsum[:, h, :], x_sum[:, h, :]))
                for t in range(TOK):
                    s = x_p[:, h, SEQ * t:SEQ * t + SEQ]
                    last = nc.vector.tensor_scalar(s, s, x_rsum[:, h, t:t + 1], None, ALU.mult)
                last.then_inc(x_normed, 1)
            for h in range(XH):
                dve.wait_ge(x_t, h + 1)
                nc.vector.tensor_copy(x_pT[:, h, :], bank[(7, 4)[h % 2]][:, :]).then_inc(x_pt, 1)
            split(35)
            for p in range(2):
                dve.wait_ge(xo_hi, p + 1)
                low(flat(aT_lo[:, 2 * p:2 * p + 2, :]), bank[p][:, :], flat(aT_hi[:, 2 * p:2 * p + 2, :]))\
                    .then_inc(xo_lo, 1)
            split(36)
            split(37)
            add_residual(1, XO0 + 2, (2, 3, 5, 6), x2_ready)
            split(38)
            for k in range(KT):
                low_T(X2, k, hT_hi, hT_lo, G_MLP)
            split(39)
            for t in range(TOK):
                last = sum_squares(xs[:, t, :], res[:, t, :], X2, t)
            step(last)
            step(nc.vector.tensor_scalar(var[:, X2, :], stat[:, X2, :], 1.0 / D, EPS, ALU.mult, ALU.add))
            step(nc.vector.reciprocal(rstd[:, X2, :], var[:, X2, :]))

            def square_low(b, n):
                dve.wait_ge(u_relu, n)
                nc.vector.tensor_tensor(relu2[:, b, :], relu[:, b, :], relu[:, b, :], ALU.mult).then_inc(u_sq, 1)
                dve.wait_ge(u_sq, n)
                dve.wait_ge(u_hi, n)
                low(flat(aT_lo[:, 4 + 2 * b:6 + 2 * b, :]), relu2[:, b, :], flat(aT_hi[:, 4 + 2 * b:6 + 2 * b, :]))\
                    .then_inc(u_lo, 1)

            square_low(0, 1)
            square_low(1, 2)
            with dve.Fori(0, ITERS) as i:
                for j in range(2):
                    for s in (2 * j + 1, 2 * j + 2):
                        c = LOOP0 + s
                        split_lo(c % RING, c % RAW, 4 * i + (c + 1))
                    square_low(j, 2 * i + (j + 3))
            for t in range(TOK):
                wait_tile(t, 2, LAST + 1)
                for c in range(2):
                    s = res[:, t, 512 * c:512 * c + 512]
                    last = nc.vector.scalar_tensor_tensor(s, bank[(2, 3, 5, 6)[2 * t + c]][:, :],
                                                          rstd[:, X2, t:t + 1], s, ALU.mult, ALU.add)
                last.then_inc(x3_ready, 1)
            dve.wait_ge(x3_ready, TOK)
            sum_squares(xs[:, 1, :], res[:, 1, :], X3, 1).then_inc(sumsq_dve, 1)
            dve.wait_ge(gfin_in, 16)
            for t in range(TOK):
                dve.wait_ge(rstd_ready, 4 + t)
                nc.vector.scalar_tensor_tensor(xs[:, t, :], res[:, t, :], rstd[:, X3, t:t + 1], gfin[:, :], ALU.mult,
                                               ALU.mult).then_inc(fin, 1)

        @block.tensor
        def _(pe):
            mm, tr = nc.tensor.matmul, nc.tensor.transpose

            def weights_T(slot, xh, xl, k0, nk, outs, used, kt_wait=None):
                cols = CH // nk
                pe.wait_ge(w_lo_ready, used)
                order = [(k, m) for m in range(len(outs)) for k in range(nk)]
                if kt_wait:
                    order = [(k, m) for k in range(nk) for m in range(len(outs))]
                for k, m in order:
                    if kt_wait and m == 0:
                        kt_wait(k)
                    at_ = k * cols + m * P
                    wh, wl = w_hi[:, slot, at_:at_ + P], w_lo[:, slot, at_:at_ + P]
                    first = k == 0 and (m == 0 or not kt_wait)
                    for n, (w, v) in enumerate(((wh, xh), (wh, xl), (wl, xh))):
                        last = mm(outs[m], w, v[:, k0 + k, :], start=first and n == 0, stop=k == nk - 1 and n == 2,
                                  skip_group_check=bool(kt_wait))
                last.then_inc(w_used, 1)

            def weights_move(slot, xh, xl, k0, nk, outs, used, start, stop, tiles=False):
                cols = CH // nk
                pe.wait_ge(w_lo_ready, used)
                for t in range(TOK):
                    for k in range(nk):
                        sh, sl = xh[:, k0 + k, t * P:(t + 1) * P], xl[:, k0 + k, t * P:(t + 1) * P]
                        for n, (s, w) in enumerate(((sh, w_hi), (sh, w_lo), (sl, w_hi))):
                            for c in range(cols // 512):
                                last = mm(outs[t][c], s, w[:, slot, k * cols + 512 * c:k * cols + 512 * c + 512],
                                          start=start and k == 0 and n == 0, stop=stop and k == nk - 1 and n == 2)
                    if tiles and t == 0:
                        last.then_inc(tile_done, 1)
                last.then_inc(w_used, 1)

            def halves(b):
                return [bank[b][:, 0:SEQ], bank[b][:, SEQ:2 * SEQ]]

            def transpose_stream(n, src, before=None):
                for k in range(KT):
                    if before:
                        before(k)
                    for t in range(TOK):
                        last = tr(t_tile(n, k)[:, t * P:(t + 1) * P], src[:, t, k * P:(k + 1) * P], ident[:, :])
                    last.then_inc(transposed[n], 1)

            pe.wait_ge(ident_ready, 1)
            pe.wait_ge(g_in, 64)
            tr(bank[7][:, 256:288], g_rows[:, :], ident[0:32, 0:32]).then_inc(gT_done, 1)
            pe.wait_ge(xs_act, 1)
            pe.wait_ge(xs_dve, 1)
            transpose_stream(X, xs, lambda k: pe.wait_ge(gT_ready, 1) if k == KT - 1 else None)

            for j in range(4):
                weights_T(j, hT_hi, hT_lo, 0, KT, halves(j), j + 1,
                          (lambda k: pe.wait_ge(lo_done[X], k + 1)) if j == 0 else None)
            for j in range(4):
                pe.wait_ge(qk_evac, j + 1)
                weights_T(j, hT_hi, hT_lo, 0, KT, halves(j), 4 + j + 1)

            for b in range(2):
                pe.wait_ge(qk_evac, 4 + 2 * b + 2)
                for j in range(2):
                    c = 8 + 2 * b + j
                    weights_move(c % RING, hT_hi, hT_lo, 4 * j, 4, [[bank[2 * b]], [bank[2 * b + 1]]], c + 1,
                                 j == 0, j == 1)
                    if c == 8:
                        pe.wait_ge(mem_scaled, TOK)
                        transpose_stream(MEM, mem_tok, lambda k: pe.wait_ge(lo_done[X], KT) if k == 0 else None)

            pe.wait_ge(lo_done[MEM], KT)
            for h in range(HEADS):
                c = GATE0 + h
                r = slice(DH * (h % 2), DH * (h % 2) + DH)
                q, k = qkT[r, h // 2, :], qkT[r, 4 + h // 2, :]
                s = bank[MO_S]
                if h:
                    pe.wait_ge(mo_biased, h)
                else:
                    pe.wait_ge(v_evac, 4)
                mm(s[:, 0:128], q[:, 0:P], k[:, 0:P], start=True, stop=True)
                mm(s[:, 128:384], q[:, P:SEQ], k, start=True, stop=True).then_inc(mo_s, 1)
                q, k = qkT[r, 8 + h // 2, :], qkT[r, 12 + h // 2, :]
                z = bank[SB_Z[h % 2]]
                if h >= 2:
                    pe.wait_ge(sb_exp, h - 1)
                mm(z[:, 0:256], k[:, 0:P], q, start=True, stop=False, skip_group_check=True)
                mm(z[:, 256:384], k[:, P:SEQ], q[:, P:SEQ], start=False, stop=False, skip_group_check=True)
                if h == 0:
                    pe.wait_ge(masks_ready, 2)
                mm(z[:, 0:384].rearrange("p (b q) -> p b q", b=3)[:, 0:3:2, :], ident_r[:, :], future_r[:, :, :],
                   start=False, stop=False, skip_group_check=True).then_inc(sb_z, 1)

                if h >= 2:
                    pe.wait_ge(gate_evac, h - 1)
                g = halves(h % 2)
                pe.wait_ge(w_lo_ready, c + 1)
                for m in range(2):
                    for kk in range(KT):
                        a = kk * 256 + m * P
                        wh, wl = w_hi[:, c % RING, a:a + P], w_lo[:, c % RING, a:a + P]
                        for n, (w, v) in enumerate(((wh, hT_hi), (wh, hT_lo), (wl, hT_hi))):
                            last = mm(g[m], w, v[:, kk, :], start=kk == 0 and n == 0, stop=kk == KT - 1 and n == 2)
                    if m == 0:
                        pe.wait_ge(sb_raw, h + 1)
                        sp_ = sb_sp[:, h % 2, :]
                        mm(z[:, 0:256], neg_tri[:, :], sp_[:, 0:256], start=False, stop=False, skip_group_check=True)
                        mm(z[:, 128:256], neg_ones[:, :], sp_[:, 256:384], start=False, stop=False,
                           skip_group_check=True)
                        mm(z[:, 256:384], neg_tri[:, :], sp_[:, 256:384], start=False, stop=True,
                           skip_group_check=True).then_inc(sb_c, 1)
                        pe.wait_ge(mo_normed, h + 1)
                        if h:
                            pe.wait_ge(mo_pt, h)
                        for j in range(3):
                            last = tr(bank[MO_PT][:, P * j:P * j + P], mo_u[:, h % 2, P * j:P * j + P], ident[:, :])
                        last.then_inc(mo_t, 1)
                last.then_inc(w_used, 1)

                pe.wait_ge(mo_pt, h + 1)
                if h >= 2 and h % 2 == 0:
                    pe.wait_ge(att_lo, h)
                for b, (o, a_, done) in enumerate(((bank[MO_O], mo_pT, mo_av), (bank[SB_O], sb_aT, sb_av))):
                    if b == 1:
                        pe.wait_ge(sb_exp, h + 1)
                    v0 = b * WIDTH + DH * h
                    a_ = a_[:, h % 2, :]
                    mm(o[r, 0:256], v_tok[:, 0, v0:v0 + DH], a_[:, 0:256], start=True, stop=False)
                    mm(o[r, 128:256], v_tok[:, 1, v0:v0 + DH], a_[:, 256:384], start=False, stop=True)\
                        .then_inc(done, 1)

            pe.wait_ge(gate_evac, 8)
            weights_T(MK[0] % RING, mT_hi, mT_lo, 0, KT, halves(0), MK[0] + 1)

            pe.wait_ge(mk_evac, 1)
            pe.wait_ge(att_lo, 8)
            for n in range(2):
                for b in range(2):
                    c = BR0 + 2 * n + b
                    o = 4 * n + 2 * b
                    if c == BR0 + 1:
                        pe.wait_ge(mo_pt, HEADS)
                    if c == BR0 + 2:
                        pe.wait_ge(sb_exp, HEADS)
                    weights_T(c % RING, aT_hi, aT_lo, 4 * b, 4, halves(o) + halves(o + 1), c + 1)

            for j in range(4):
                c = OUT0 + j
                pe.wait_ge(mix_lo, j + 1)
                if j == 0:
                    pe.wait_ge(mixed, 2)
                weights_move(c % RING, mixT_hi, mixT_lo, 2 * j, 2, [[bank[0], bank[1]], [bank[2], bank[3]]], c + 1,
                             j == 0, j == 3, tiles=j == 3)

            pe.wait_ge(mix_lo, 4)
            weights_T(MK[1] % RING, mT_hi, mT_lo, 0, KT, halves(4), MK[1] + 1)
            pe.wait_ge(x1_ready, TOK)
            transpose_stream(X1, res)
            mv_out = [[bank[5]], [bank[6]]]
            weights_move(MV[0] % RING, mT_hi, mT_lo, 0, 4, mv_out, MV[0] + 1, True, False)

            pe.wait_ge(lo_done[X1], KT)
            pe.wait_ge(mk_evac, 2)
            for j in range(2):
                weights_T((XQ0 + j) % RING, hT_hi, hT_lo, 0, KT, halves((7, 4)[j]), XQ0 + j + 1)
            for h in range(XH):
                pe.wait_ge(xq_evac, h // 2 + 1)
                for t in range(TOK):
                    last = mm(bank[h][:, SEQ * t:SEQ * t + SEQ], xqT[:, h, t * P:(t + 1) * P], mkT[:, h, :],
                              start=True, stop=True)
                last.then_inc(x_s, 1)
            weights_move(MV[1] % RING, mT_hi, mT_lo, 4, 4, mv_out, MV[1] + 1, False, True)
            for h in range(XH):
                pe.wait_ge(x_normed, h + 1)
                if h >= 2:
                    pe.wait_ge(x_pt, h - 1)
                b_ = bank[(7, 4)[h % 2]]
                for kt in range(2):
                    for t in range(TOK):
                        last = tr(b_[:, SEQ * kt + P * t:SEQ * kt + P * t + P],
                                  x_p[:, h, SEQ * t + P * kt:SEQ * t + P * kt + P], ident[:, :])
                last.then_inc(x_t, 1)
            pe.wait_ge(mv_evac, TOK)
            for h in range(XH):
                pe.wait_ge(x_pt, h + 1)
                for kt in range(2):
                    last = mm(bank[h // 2][:, SEQ * (h % 2):SEQ * (h % 2) + SEQ], mv_tok[:, kt, XDH * h:XDH * h + XDH],
                              x_pT[:, h, SEQ * kt:SEQ * kt + SEQ], start=kt == 0, stop=kt == 1)
                last.then_inc(x_av, 1)

            acc = [[bank[2], bank[3]], [bank[5], bank[6]]]
            for j in range(2):
                pe.wait_ge(xo_lo, j + 1)
                weights_move((XO0 + j) % RING, aT_hi, aT_lo, 2 * j, 2, acc, XO0 + j + 1, j == 0, j == 1, tiles=j == 1)
            pe.wait_ge(x2_ready, TOK)
            transpose_stream(X2, res)

            def up(b, slot, used, relus, kt_wait=None):
                if relus is not None:
                    pe.wait_ge(u_relu, relus)
                weights_T(slot, hT_hi, hT_lo, 0, KT, halves(b), used, kt_wait)

            def down(b, slot, used, lows, start=False, stop=False):
                pe.wait_ge(u_lo, lows)
                weights_move(slot, aT_hi, aT_lo, 4 + 2 * b, 2, acc, used, start, stop, tiles=stop)

            pe.wait_ge(lo_done[X2], KT)
            up(0, UP0 % RING, UP0 + 1, None)
            up(1, (UP0 + 1) % RING, UP0 + 2, None)
            down(0, (UP0 + 2) % RING, UP0 + 3, 1, start=True)
            with pe.Fori(0, ITERS) as i:
                for j in range(2):
                    c = LOOP0 + 2 * j
                    up(j, c % RING, 4 * i + (c + 1), 2 * i + (j + 1))
                    down(1 - j, (c + 1) % RING, 4 * i + (c + 2), 2 * i + (j + 2))
            down((PAIRS - 1) % 2, LAST % RING, LAST + 1, PAIRS, stop=True)


_INS = ['x', 'mem', 'g_mix', 'w_in', 'w_br_moba', 'w_br_sb', 'w_out', 'g_cross', 'g_mem', 'w_xq', 'w_xkv', 'w_xo',
        'g_mlp', 'w_up', 'w_down', 'g_final']


def kernel(**inputs):
    import numpy as np
    import concourse.bacc as bacc
    from concourse.bass_utils import run_bass_kernel_spmd

    nc = bacc.Bacc("TRN2", target_bir_lowering=False, num_devices=1)
    arrays, args = {}, []
    for name in _INS:
        a = np.ascontiguousarray(inputs[name])
        arrays[f"in_{name}_dram"] = a
        args.append(nc.dram_tensor(f"in_{name}_dram", a.shape, mybir.dt.from_np(a.dtype), kind="ExternalInput").ap())
    shape = inputs["x"].shape
    args.append(nc.dram_tensor("out_dram", shape, mybir.dt.float32, kind="ExternalOutput").ap())
    hybrid_layer(nc, *args)
    return run_bass_kernel_spmd(nc, [arrays], core_ids=[0]).results[0]["out_dram"]
```

```python
import concourse.bass as bass
from concourse import mybir
from contextlib import ExitStack

P = 128


def hybrid_layer(nc, x, mem, g_mix, w_in, w_br_moba, w_br_sb, w_out, g_cross, g_mem,
                 w_xq, w_xkv, w_xo, g_mlp, w_up, w_down, g_final, out):
    fp32, f32r = mybir.dt.float32, mybir.dt.float32r
    ACT, ALU = mybir.ActivationFunctionType, mybir.AluOpType
    AX = mybir.AxisListType.X

    SEQ, D = x.shape[1], x.shape[2]
    TOK = SEQ // P
    KT = D // P
    HEADS, DH = 8, 64
    WIDTH = HEADS * DH
    XH, XDH = 4, 128
    XW = XH * XDH
    FF = w_up.shape[2]
    RING, RAW = 4, 2
    CH = 2048
    PAIRS = FF // (2 * P)
    EPS, NEG = 1e-6, -1e30
    assert (SEQ, TOK, KT) == (256, 2, 8)

    def by_cols(w, k0, nk, c0, nc_):
        return w[0, k0 * P:(k0 + nk) * P, c0:c0 + nc_].rearrange("(k p) n -> p k n", p=P)

    QKV = 3 * WIDTH
    stream = []
    for base in (0, QKV):
        stream += [by_cols(w_in, 0, 8, base + 256 * j, 256) for j in range(4)]
    for base in (2 * WIDTH, QKV + 2 * WIDTH):
        stream += [by_cols(w_in, 4 * j, 4, base, 512) for j in range(2)]
    GATE0 = len(stream)
    stream += [by_cols(w_in, 0, 8, 2 * QKV + 256 * j, 256) for j in range(8)]
    mem_k = [by_cols(w_xkv, 0, 8, 256 * j, 256) for j in range(2)]
    mem_v = [by_cols(w_xkv, 4 * j, 4, XW, 512) for j in range(2)]
    MK = [len(stream)]
    stream.append(mem_k[0])
    BR0 = len(stream)
    for n in range(2):
        stream += [by_cols(w, 0, 4, 512 * n, 512) for w in (w_br_moba, w_br_sb)]
    OUT0 = len(stream)
    stream += [by_cols(w_out, 2 * j, 2, 0, 1024) for j in range(4)]
    MK.append(len(stream))
    MV = [len(stream) + 1, len(stream) + 4]
    XQ0 = len(stream) + 2
    stream += [mem_k[1], mem_v[0]] + [by_cols(w_xq, 0, 8, 256 * j, 256) for j in range(2)] + [mem_v[1]]
    XO0 = len(stream)
    stream += [by_cols(w_xo, 2 * j, 2, 0, 1024) for j in range(2)]
    UP0 = len(stream)
    stream += [by_cols(w_up, 0, 8, 0, 256), by_cols(w_up, 0, 8, 256, 256), by_cols(w_down, 0, 2, 0, 1024)]
    LOOP0 = len(stream)
    ITERS = (PAIRS - 2) // 2
    LAST = LOOP0 + 4 * ITERS
    assert LOOP0 == 39 and LAST == 67 and PAIRS == 2 * ITERS + 2

    def up_cols(i):
        return w_up[0, :, bass.ds(i * 256, 256)].rearrange("(k p) n -> p k n", p=P)

    def down_rows(i):
        return w_down[0, bass.ds(i * 256, 256), :].rearrange("(k p) n -> p k n", p=P)

    ctx = ExitStack()
    with ctx:
        at = [(nc.sbuf_base + 31) // 32 * 32]

        def place(name, shape, dt=fp32, over=None):
            size = 4
            for s in shape[1:]:
                size *= s
            offset = at[0] if over is None else over
            t = nc.alloc_sbuf_tensor_at(name, shape, dt, offset=offset)
            if over is None:
                at[0] += (size + 31) // 32 * 32
            return t, offset

        def sb(name, shape, dt=fp32, over=None):
            return place(name, shape, dt, over)[0]

        def sem(name):
            return ctx.enter_context(nc.semaphore(name))

        raw = sb("raw", [P, RAW, CH])
        w_hi = sb("w_hi", [P, RING, CH], f32r)
        w_lo = sb("w_lo", [P, RING, CH], f32r)
        res = sb("res", [P, TOK, D])
        hT_hi = sb("hT_hi", [P, KT, SEQ], f32r)
        hT_lo = sb("hT_lo", [P, KT, SEQ], f32r)
        mT_hi = sb("mT_hi", [P, KT, SEQ], f32r)
        mT_lo = sb("mT_lo", [P, KT, SEQ], f32r)
        qkT, o = place("qkT", [P, 16, SEQ])
        mixT_hi = sb("mixT_hi", [P, KT, SEQ], f32r, over=o)
        mixT_lo = sb("mixT_lo", [P, KT, SEQ], f32r, over=o + 8192)
        xqT = sb("xqT", [P, XH, SEQ], over=o)
        v_tok, o = place("v_tok", [P, TOK, 2 * WIDTH])
        mkT = sb("mkT", [P, XH, SEQ], over=o)
        mv_tok = sb("mv_tok", [P, TOK, XW], over=o + 4096)
        gfin = sb("gfin", [P, D], over=o)
        gateT, o = place("gateT", [P, 16, SEQ])
        xs = sb("xs", [P, TOK, D], over=o)
        mem_tok = sb("mem_tok", [P, TOK, D], over=o + 8192)
        aT_hi = sb("aT_hi", [P, 8, SEQ], f32r)
        aT_lo = sb("aT_lo", [P, 8, SEQ], f32r)
        alibi, o = place("alibi", [P, HEADS, SEQ])
        mo_u = sb("mo_u", [P, 2, 384])
        mo_pT = sb("mo_pT", [P, 2, 384])
        sb_aT = sb("sb_aT", [P, 2, 384])
        sb_t = sb("sb_t", [P, 384])
        sb_sp = sb("sb_sp", [P, 2, 384])
        gated_a = sb("gated_a", [P, 2, 512], over=o)
        gated_b = sb("gated_b", [P, 2, 512], over=o + 4096)
        x_p = sb("x_p", [P, XH, 512], over=o)
        x_pT = sb("x_pT", [P, XH, 512], over=o + 8192)
        relu = sb("relu", [P, 2, 512], over=o)
        relu2 = sb("relu2", [P, 2, 512], over=o + 4096)
        ident = sb("ident", [P, P])
        neg_tri = sb("neg_tri", [P, P])
        neg_ones = sb("neg_ones", [P, P])
        ident_r = sb("ident_r", [P, P], f32r)
        future_r = sb("future_r", [P, 2, P], f32r)
        g_mix_rows = sb("g_mix_rows", [8, P])
        g_rows = sb("g_rows", [24, P])
        gT = sb("gT", [P, 32])
        rstd_diag = sb("rstd_diag", [P, SEQ])
        rstd_row = sb("rstd_row", [P, 2, SEQ])
        half = sb("half", [P, 2])
        stat = sb("stat", [P, 5, 2])
        var = sb("var", [P, 5, 2])
        rstd = sb("rstd", [P, 5, 2])
        mo_max = sb("mo_max", [P, 2])
        mo_nmax = sb("mo_nmax", [P, 2])
        mo_sum = sb("mo_sum", [P, 2])
        mo_rsum = sb("mo_rsum", [P, 2])
        x3_ms = sb("x3_ms", [P, TOK, 2])
        x_scale = sb("x_scale", [P, 2])
        x_max = sb("x_max", [P, XH, 2])
        x_bias = sb("x_bias", [P, XH, 2])
        x_sum = sb("x_sum", [P, XH, 2])
        x_rsum = sb("x_rsum", [P, XH, 2])
        assert at[0] <= nc.sbuf_usable_end
        X, MEM, X1, X2, X3 = range(5)
        G_MIX, G_CROSS, G_MEM, G_MLP = range(0, 32, 8)

        bank = [ctx.enter_context(nc.psum_tensor(f"bank{i}", [P, 512], fp32))[:, :] for i in range(8)]
        MO_S, MO_PT, SB_Z, MO_O, SB_O = 2, 3, (4, 5), 6, 7

        x_in = [sem(f"x_in{t}") for t in range(TOK)]
        g_mix_in, g_in, first_in, first_hi, first_lo = (sem(n) for n in ("g_mix_in", "g_in", "first_in", "first_hi",
                                                                         "first_lo"))
        diag_ready, row_done, row_ready = sem("diag_ready"), sem("row_done"), sem("row_ready")
        mem_in, gfin_in = sem("mem_in"), sem("gfin_in")
        raw_in = [sem(f"raw_in{s}") for s in range(RAW)]
        stored = sem("stored")
        ident_ready, masks_ready, alibi_ready = sem("ident_ready"), sem("masks_ready"), sem("alibi_ready")
        pool_step, dve_step = sem("pool_step"), sem("dve_step")
        w_hi_ready, w_lo_ready, w_used = sem("w_hi_ready"), sem("w_lo_ready"), sem("w_used")
        half_ready, sumsq_act, sumsq_dve = sem("half_ready"), sem("sumsq_act"), sem("sumsq_dve")
        rstd_ready = sem("rstd_ready")
        mem_scaled = sem("mem_scaled")
        gT_done, gT_ready = sem("gT_done"), sem("gT_ready")
        NAMES = {X: "x", MEM: "mem", X1: "x1", X2: "x2"}
        transposed = {n: sem(f"{s}_transposed") for n, s in NAMES.items()}
        hi_done = {n: sem(f"{s}_hi_done") for n, s in NAMES.items()}
        lo_done = {n: sem(f"{s}_lo_done") for n, s in NAMES.items()}
        qk_evac, v_evac, gate_evac = sem("qk_evac"), sem("v_evac"), sem("gate_evac")
        mo_s, mo_biased, mo_exp, mo_normed = sem("mo_s"), sem("mo_biased"), sem("mo_exp"), sem("mo_normed")
        mo_t, mo_pt, mo_av = sem("mo_t"), sem("mo_pt"), sem("mo_av")
        sb_z, sb_abs, sb_e, sb_ln = sem("sb_z"), sem("sb_abs"), sem("sb_e"), sem("sb_ln")
        sb_raw, sb_c = sem("sb_raw"), sem("sb_c")
        sb_exp, sb_av = sem("sb_exp"), sem("sb_av")
        att_hi, att_lo = sem("att_hi"), sem("att_lo")
        sig_ready = sem("sig_ready")
        mixed, mix_hi, mix_lo = sem("mixed"), sem("mix_hi"), sem("mix_lo")
        x1_ready, x2_ready = sem("x1_ready"), sem("x2_ready")
        mk_evac, mv_evac, xq_evac = sem("mk_evac"), sem("mv_evac"), sem("xq_evac")
        x_s, x_biased, x_exp, x_normed = sem("x_s"), sem("x_biased"), sem("x_exp"), sem("x_normed")
        x_t, x_pt, x_av, xo_hi, xo_lo = sem("x_t"), sem("x_pt"), sem("x_av"), sem("xo_hi"), sem("xo_lo")
        u_relu, u_sq, u_hi, u_lo = sem("u_relu"), sem("u_sq"), sem("u_hi"), sem("u_lo")
        tile_done, x3_ready, fin = sem("tile_done"), sem("x3_ready"), sem("fin")

        block = ctx.enter_context(nc.Block())

        @block.sync
        def _(sp):
            def load(c, src, slot, used=None):
                if used is not None:
                    sp.wait_ge(w_lo_ready, used)
                sp.dma_start(raw[:, slot, :].rearrange("p (k n) -> p k n", k=src.shape[1]), src)\
                    .then_inc(raw_in[slot], 16)

            for t in range(TOK):
                sp.dma_start(res[:, t, :], x[0, t * P:(t + 1) * P, :]).then_inc(x_in[t], 16)
            first = raw[:, 0, :].rearrange("p (k n) -> p k n", k=KT)
            sp.dma_start(first[:, 0:4, :], stream[0][:, 0:4, :]).then_inc(first_in, 16)
            sp.dma_start(first[:, 4:8, :], stream[0][:, 4:8, :]).then_inc(raw_in[0], 16)
            load(1, stream[1], 1)
            sp.dma_start(mem_tok[:, :, :], mem[0, :, :].rearrange("(t p) d -> p t d", p=P)).then_inc(mem_in, 16)
            for c in range(RAW, LOOP0):
                load(c, stream[c], c % RAW, c - RAW + 1)
            with sp.Fori(0, ITERS) as i:
                for j in range(4):
                    src = (up_cols if j % 2 == 0 else down_rows)(2 * i + (2 + j // 2 if j % 2 == 0 else 1 + j // 2))
                    load(None, src, (LOOP0 + j) % RAW, 4 * i + (LOOP0 + j - RAW + 1))
            load(LAST, by_cols(w_down, 2 * (PAIRS - 1), 2, 0, 1024), LAST % RAW, LAST - RAW + 1)
            sp.wait_ge(x_av, XH)
            sp.dma_start(gfin[:, :], g_final.rearrange("(a d) -> a d", a=1).to_broadcast([P, D])).then_inc(gfin_in, 16)
            for t in range(TOK):
                sp.wait_ge(fin, t + 1)
                sp.dma_start(out[0, t * P:(t + 1) * P, :], xs[:, t, :]).then_inc(stored, 16)
            sp.wait_ge(stored, 16 * TOK)

        @block.gpsimd
        def _(pool):
            steps = [0]

            def step(ins):
                steps[0] += 1
                ins.then_inc(pool_step, 1)
                pool.wait_ge(pool_step, steps[0])

            nc.gpsimd.memset(half[:, :], -0.5).then_inc(half_ready, 1)
            step(nc.gpsimd.memset(ident[:, :], 0.0))
            nc.gpsimd.affine_select(out=ident[:, :], in_=ident[:, :], compare_op=ALU.not_equal, fill=1.0, base=0,
                                    pattern=[[-1, P]], channel_multiplier=1).then_inc(ident_ready, 1)

            def rsqrt(n, t0=0, t1=TOK):
                step(nc.gpsimd.tensor_scalar(var[:, n, t0:t1], stat[:, n, t0:t1], 1.0 / D, EPS, ALU.mult, ALU.add))
                nc.gpsimd.tensor_tensor(rstd[:, n, t0:t1], var[:, n, t0:t1], half[:, t0:t1], ALU.pow)\
                    .then_inc(rstd_ready, 1)

            pool.wait_ge(half_ready, 1)
            pool.wait_ge(sumsq_act, 1)
            pool.wait_ge(sumsq_dve, 1)
            rsqrt(X)
            step(nc.gpsimd.memset(neg_ones[:, :], -1.0))
            nc.gpsimd.affine_select(out=neg_tri[:, :], in_=neg_ones[:, :], compare_op=ALU.is_ge, fill=0.0, base=0,
                                    pattern=[[-1, P]], channel_multiplier=1).then_inc(masks_ready, 1)
            step(nc.gpsimd.memset(future_r[:, :, :].bitcast(fp32), 0.0))
            step(nc.gpsimd.affine_select(out=future_r[:, :, :], in_=future_r[:, :, :].bitcast(fp32),
                                         compare_op=ALU.is_gt, fill=NEG, base=0, pattern=[[0, 2], [1, P]],
                                         channel_multiplier=-1))
            nc.gpsimd.tensor_copy(ident_r[:, :], ident[:, :]).then_inc(masks_ready, 1)
            step(nc.gpsimd.iota(alibi[:, 0, :], pattern=[[1, SEQ]], base=-P, channel_multiplier=-1,
                                allow_small_or_imprecise_dtypes=True))
            for h in range(HEADS - 1, -1, -1):
                step(nc.gpsimd.tensor_scalar(alibi[:, h, :], alibi[:, 0, :], 2.0 ** (-8.0 * (h + 1) / HEADS), 0.0,
                                             ALU.mult, ALU.add))
            for h in range(HEADS):
                last = nc.gpsimd.affine_select(out=alibi[:, h, :], in_=alibi[:, h, :], compare_op=ALU.is_ge, fill=NEG,
                                               base=P, pattern=[[-1, SEQ]], channel_multiplier=1)
                last.then_inc(alibi_ready, 1)
            pool.wait_ge(sumsq_dve, 2)
            rsqrt(MEM)

            pool.wait_ge(sumsq_dve, 3)
            rsqrt(X1)
            for t in range(TOK):
                pool.wait_ge(sumsq_act, 2 * t + 3)
                step(nc.gpsimd.tensor_scalar(var[:, X3, t:t + 1], x3_ms[:, t, 0:1], x3_ms[:, t, 1:2], EPS, ALU.add,
                                             ALU.add))
                nc.gpsimd.tensor_tensor(rstd[:, X3, t:t + 1], var[:, X3, t:t + 1], half[:, 0:1], ALU.pow)\
                    .then_inc(rstd_ready, 1)

        T_BANKS = {X: (range(8), 1), MEM: ((4, 5, 6, 7), 2), X1: ((0, 1, 2, 3), 2), X2: ((0, 1, 7, 4), 2)}

        def t_tile(n, k):
            banks, per = T_BANKS[n]
            return bank[banks[k // per]][:, SEQ * (k % per):SEQ * (k % per) + SEQ]

        def bank_full(n, k):
            per = T_BANKS[n][1]
            return (k // per + 1) * per

        def flat(t):
            return t.rearrange("p b t -> p (b t)")

        @block.scalar
        def _(act):
            copy = nc.scalar.activation
            nc.scalar.preload_act_table_set("natural_log_exp_and_others")
            act.dma_start(g_mix_rows[:, :], g_mix[0, :].rearrange("(k p) -> k p", p=P)).then_inc(g_mix_in, 16)
            for j, g in enumerate((g_cross, g_mem, g_mlp)):
                act.dma_start(g_rows[8 * j:8 * j + 8, :], g[0, :].rearrange("(k p) -> k p", p=P)).then_inc(g_in, 16)

            def split_hi(slot, rslot, arrived, used=None):
                act.wait_ge(raw_in[rslot], arrived)
                if used is not None:
                    act.wait_ge(w_used, used)
                copy(w_hi[:, slot, :], raw[:, rslot, :], ACT.Copy).then_inc(w_hi_ready, 1)

            def split(c):
                split_hi(c % RING, c % RAW, 16 * (c // RAW + 1), c - RING + 1 if c >= RING else None)

            def high_T(n, k, dst, g):
                act.wait_ge(transposed[n], bank_full(n, k))
                copy(dst[:, k, :], t_tile(n, k), ACT.Copy, scale=gT[:, g + k:g + k + 1]).then_inc(hi_done[n], 1)

            act.wait_ge(x_in[0], 16)
            copy(xs[:, 0, :], res[:, 0, :], ACT.Square, accum_out=stat[:, X, 0:1]).then_inc(sumsq_act, 1)
            act.wait_ge(gT_ready, 1)
            for k in range(KT):
                high_T(X, k, hT_hi, G_MIX)
                if k == 2:
                    act.wait_ge(first_in, 16)
                    copy(w_hi[:, 0, 0:CH // 2], raw[:, 0, 0:CH // 2], ACT.Copy).then_inc(first_hi, 1)
            act.wait_ge(raw_in[0], 16)
            copy(w_hi[:, 0, CH // 2:CH], raw[:, 0, CH // 2:CH], ACT.Copy).then_inc(w_hi_ready, 1)
            for c in range(1, RING):
                split(c)
            with act.Fori(0, 2) as i:
                for j in range(4):
                    split_hi(j, j % 2, 32 * i + 16 * (j // 2 + 3), 4 * i + (j + 1))
            act.wait_ge(gT_ready, 2)
            for k in range(KT):
                high_T(MEM, k, mT_hi, G_MEM)
                if k == 3:
                    split(12)
            for b in range(2):
                act.wait_ge(w_used, 10 + 2 * b)
                for t in range(TOK):
                    copy(v_tok[:, t, b * WIDTH:(b + 1) * WIDTH], bank[2 * b + t][:, :], ACT.Copy,
                         scale=rstd[:, X, t:t + 1]).then_inc(v_evac, 1)
                split(13 + b)

            def att_high(p):
                act.wait_ge(mo_av, 2 * p + 2)
                copy(aT_hi[:, p, :], bank[MO_O][:, 0:SEQ], ACT.Copy).then_inc(att_hi, 1)
                act.wait_ge(sb_av, 2 * p + 2)
                copy(aT_hi[:, 4 + p, :], bank[SB_O][:, 0:SEQ], ACT.Copy).then_inc(att_hi, 1)

            def softplus_exp(h):
                act.wait_ge(sb_z, h + 1)
                if h:
                    act.wait_ge(sb_raw, h)
                copy(sb_t[:, :], bank[SB_Z[h % 2]][:, 0:384], ACT.Abs).then_inc(sb_abs, 1)
                act.wait_ge(sb_abs, h + 1)
                copy(sb_t[:, :], sb_t[:, :], ACT.Exp, scale=-1.0).then_inc(sb_e, 1)
                act.wait_ge(sb_e, h + 1)
                copy(sb_t[:, :], sb_t[:, :], ACT.Ln, bias=1.0).then_inc(sb_ln, 1)
                act.wait_ge(mo_biased, h + 1)
                for q, (a, b) in enumerate(((0, 128), (128, 384))):
                    last = copy(mo_u[:, h % 2, a:b], mo_u[:, h % 2, a:b], ACT.Exp, bias=mo_nmax[:, q:q + 1],
                                accum_out=mo_sum[:, q:q + 1])
                last.then_inc(mo_exp, 1)

            split(15)
            softplus_exp(0)
            for h in range(HEADS):
                act.wait_ge(sb_c, h + 1)
                if h >= 2:
                    act.wait_ge(sb_av, h - 1)
                copy(sb_aT[:, h % 2, :], bank[SB_Z[h % 2]][:, 0:384], ACT.Exp).then_inc(sb_exp, 1)
                if h + 1 < HEADS:
                    softplus_exp(h + 1)
                split(GATE0 + h + 4)
                if h % 2:
                    att_high(h // 2)
            act.wait_ge(w_used, MK[0] + 1)
            copy(flat(mkT[:, 0:2, :]), bank[0][:, :], ACT.Copy).then_inc(mk_evac, 1)
            act.wait_ge(gate_evac, 8)
            for n in range(2):
                for b in range(2):
                    s = gateT[:, 8 * b + 4 * n:8 * b + 4 * n + 4, :]
                    copy(s, s, ACT.Sigmoid).then_inc(sig_ready, 1)
                if n == 0:
                    split(24)
            for j in range(4):
                act.wait_ge(mixed, j + 1)
                copy(flat(mixT_hi[:, 2 * j:2 * j + 2, :]), gated_a[:, j % 2, :], ACT.Copy).then_inc(mix_hi, 1)
                if j == 1:
                    split(25)
                    split(26)
            for c in range(27, 32):
                split(c)
            act.wait_ge(w_used, MK[1] + 1)
            copy(flat(mkT[:, 2:4, :]), bank[4][:, :], ACT.Copy).then_inc(mk_evac, 1)
            split(32)
            for k in range(KT):
                high_T(X1, k, hT_hi, G_CROSS)
            split(33)
            for j in range(2):
                act.wait_ge(w_used, XQ0 + j + 1)
                copy(flat(xqT[:, 2 * j:2 * j + 2, :]), bank[(7, 4)[j]][:, :], ACT.Copy).then_inc(xq_evac, 1)
                if j == 0:
                    split(34)
            for h in range(XH):
                act.wait_ge(x_biased, h + 1)
                for t in range(TOK):
                    last = copy(x_p[:, h, SEQ * t:SEQ * t + SEQ], bank[h][:, SEQ * t:SEQ * t + SEQ], ACT.Exp,
                                bias=x_bias[:, h, t:t + 1], scale=x_scale[:, t:t + 1],
                                accum_out=x_sum[:, h, t:t + 1])
                last.then_inc(x_exp, 1)
                if h == 1:
                    split(35)
            act.wait_ge(w_used, MV[1] + 1)
            for t in range(TOK):
                copy(mv_tok[:, t, :], bank[5 + t][:, :], ACT.Copy).then_inc(mv_evac, 1)
            split(36)
            for p in range(2):
                act.wait_ge(x_av, 2 * p + 2)
                copy(flat(aT_hi[:, 2 * p:2 * p + 2, :]), bank[p][:, :], ACT.Copy).then_inc(xo_hi, 1)
            split(37)
            split(38)
            for k in range(KT):
                high_T(X2, k, hT_hi, G_MLP)
            split(39)

            def square_relu(b, used, relu_free, mine):
                act.wait_ge(w_used, used)
                if relu_free is not None:
                    act.wait_ge(u_sq, relu_free)
                copy(relu[:, b, :], bank[b][:, :], ACT.Relu).then_inc(u_relu, 1)
                act.wait_ge(u_relu, mine)
                copy(flat(aT_hi[:, 4 + 2 * b:6 + 2 * b, :]), relu[:, b, :], ACT.Square).then_inc(u_hi, 1)

            square_relu(0, UP0 + 1, None, 1)
            square_relu(1, UP0 + 2, None, 2)
            with act.Fori(0, ITERS) as i:
                for j in range(2):
                    for s in (2 * j + 1, 2 * j + 2):
                        c = LOOP0 + s
                        split_hi(c % RING, c % RAW, 32 * i + 16 * (c // RAW + 1), 4 * i + (c - RING + 1))
                    square_relu(j, 4 * i + (LOOP0 + 2 * j + 1), 2 * i + (j + 1), 2 * i + (j + 3))
            for t in range(TOK):
                for c in range(2):
                    act.wait_ge(x3_ready, 2 * t + c + 1)
                    copy((relu, relu2)[t][:, c, :], res[:, t, 512 * c:512 * c + 512], ACT.Square, scale=D ** -0.5,
                         accum_out=x3_ms[:, t, c:c + 1]).then_inc(sumsq_act, 1)

        @block.vector
        def _(dve):
            steps = [0]

            def step(ins):
                steps[0] += 1
                ins.then_inc(dve_step, 1)
                dve.wait_ge(dve_step, steps[0])

            sub = ALU.subtract

            def low(dst, whole, high):
                return nc.vector.tensor_tensor(dst, whole, high.bitcast(fp32), sub)

            def split_lo(slot, rslot, hi):
                dve.wait_ge(w_hi_ready, hi)
                low(w_lo[:, slot, :], raw[:, rslot, :], w_hi[:, slot, :]).then_inc(w_lo_ready, 1)

            def split(c):
                split_lo(c % RING, c % RAW, c + 1)

            def low_T(n, k, hi, lo, g):
                dve.wait_ge(hi_done[n], bank_full(n, k))
                nc.vector.scalar_tensor_tensor(lo[:, k, :], t_tile(n, k), gT[:, g + k:g + k + 1],
                                               hi[:, k, :].bitcast(fp32), ALU.mult, sub).then_inc(lo_done[n], 1)

            def sum_squares(scratch, src, n, t):
                return nc.vector.tensor_tensor_reduce(out=scratch, in0=src, in1=src, scale=1.0, scalar=0.0,
                                                      op0=ALU.mult, op1=ALU.add, accum_out=stat[:, n, t:t + 1])

            dve.wait_ge(gT_done, 1)
            nc.vector.tensor_copy(gT[:, 0:8], bank[7][:, 256:264]).then_inc(gT_ready, 1)
            dve.wait_ge(x_in[1], 16)
            sum_squares(xs[:, 1, :], res[:, 1, :], X, 1).then_inc(sumsq_dve, 1)
            for k in range(KT):
                low_T(X, k, hT_hi, hT_lo, G_MIX)
                if k == 2:
                    dve.wait_ge(first_hi, 1)
                    low(w_lo[:, 0, 0:CH // 2], raw[:, 0, 0:CH // 2], w_hi[:, 0, 0:CH // 2]).then_inc(first_lo, 1)
            dve.wait_ge(w_hi_ready, 1)
            low(w_lo[:, 0, CH // 2:CH], raw[:, 0, CH // 2:CH], w_hi[:, 0, CH // 2:CH]).then_inc(w_lo_ready, 1)
            dve.wait_ge(rstd_ready, 1)
            dve.wait_ge(ident_ready, 1)
            for t in range(TOK):
                last = nc.vector.tensor_scalar(rstd_diag[:, t * P:(t + 1) * P], ident[:, :], rstd[:, X, t:t + 1], -1.0,
                                               ALU.mult, ALU.mult)
            last.then_inc(diag_ready, 1)
            for c in range(1, RING):
                split(c)
                if c == 1:
                    dve.wait_ge(row_done, 1)
                    for j in range(2):
                        last = nc.vector.tensor_copy(rstd_row[:, j, :], bank[6][:, 0:SEQ])
                    last.then_inc(row_ready, 1)
            dve.wait_ge(mem_in, 16)
            for t in range(TOK):
                last = sum_squares(xs[:, t, :], mem_tok[:, t, :], MEM, t)
            last.then_inc(sumsq_dve, 1)
            dve.wait_ge(row_ready, 1)
            with dve.Fori(0, 2) as i:
                for j in range(4):
                    dve.wait_ge(w_used, 4 * i + (j + 1))
                    nc.vector.scalar_tensor_tensor(flat(qkT[:, bass.ds(8 * i + 2 * j, 2), :]), bank[j][:, :],
                                                   DH ** -0.5 if j < 2 else 1.0, flat(rstd_row[:, :, :]),
                                                   ALU.mult, ALU.mult).then_inc(qk_evac, 1)
                    split_lo(j, j % 2, 4 * i + (j + 5))
            dve.wait_ge(gT_done, 2)
            nc.vector.tensor_copy(gT[:, 8:32], bank[4][:, 0:24]).then_inc(gT_ready, 1)
            dve.wait_ge(rstd_ready, 2)
            for t in range(TOK):
                nc.vector.tensor_scalar(mem_tok[:, t, :], mem_tok[:, t, :], rstd[:, MEM, t:t + 1], None, ALU.mult)\
                    .then_inc(mem_scaled, 1)
            for k in range(KT):
                low_T(MEM, k, mT_hi, mT_lo, G_MEM)
                if k == 3:
                    split(12)
            split(13)
            split(14)
            split(15)

            def att_low(p):
                for b, o in enumerate((MO_O, SB_O)):
                    dve.wait_ge(att_hi, 2 * p + b + 1)
                    low(aT_lo[:, 4 * b + p, :], bank[o][:, 0:SEQ], aT_hi[:, 4 * b + p, :]).then_inc(att_lo, 1)

            def scores(h):
                dve.wait_ge(mo_s, h + 1)
                if h >= 2:
                    dve.wait_ge(mo_t, h - 1)
                for q, (a, b, c) in enumerate(((0, 128, 128), (128, 384, 0))):
                    last = nc.vector.tensor_tensor_reduce(out=mo_u[:, h % 2, a:b], in0=bank[MO_S][:, a:b],
                                                          in1=alibi[:, h, c:SEQ], scale=1.0, scalar=-3e38,
                                                          op0=ALU.add, op1=ALU.max, accum_out=mo_max[:, q:q + 1])
                step(last)
                nc.vector.tensor_scalar(mo_nmax[:, :], mo_max[:, :], -1.0, None, ALU.mult).then_inc(mo_biased, 1)
                dve.wait_ge(sb_ln, h + 1)
                if h >= 2:
                    dve.wait_ge(sb_c, h - 1)
                nc.vector.scalar_tensor_tensor(sb_sp[:, h % 2, :], bank[SB_Z[h % 2]][:, 0:384], 0.0, sb_t[:, :],
                                               ALU.max, ALU.add).then_inc(sb_raw, 1)
                dve.wait_ge(mo_exp, h + 1)
                step(nc.vector.reciprocal(mo_rsum[:, :], mo_sum[:, :]))
                for q, (a, b) in enumerate(((0, 128), (128, 384))):
                    last = nc.vector.tensor_scalar(mo_u[:, h % 2, a:b], mo_u[:, h % 2, a:b], mo_rsum[:, q:q + 1], None,
                                                   ALU.mult)
                last.then_inc(mo_normed, 1)

            dve.wait_ge(alibi_ready, HEADS)
            scores(0)
            for h in range(HEADS):
                dve.wait_ge(mo_t, h + 1)
                if h >= 2:
                    dve.wait_ge(mo_av, h - 1)
                nc.vector.tensor_copy(mo_pT[:, h % 2, :], bank[MO_PT][:, 0:384]).then_inc(mo_pt, 1)
                if h + 1 < HEADS:
                    scores(h + 1)
                dve.wait_ge(w_used, GATE0 + h + 1)
                nc.vector.tensor_tensor(flat(gateT[:, 2 * h:2 * h + 2, :]), bank[h % 2][:, :],
                                        flat(rstd_row[:, :, :]), ALU.mult).then_inc(gate_evac, 1)
                split(GATE0 + h + 4)
                if h % 2:
                    att_low(h // 2)
            split(24)
            for j in range(4):
                n, jj = j // 2, j % 2
                dve.wait_ge(w_used, BR0 + 2 * n + 1)
                dve.wait_ge(sig_ready, 2 * n + 1)
                if j >= 2:
                    dve.wait_ge(mix_hi, j - 1)
                nc.vector.tensor_tensor(gated_a[:, jj, :], bank[4 * n + jj][:, :], flat(gateT[:, 2 * j:2 * j + 2, :]),
                                        ALU.mult)
                dve.wait_ge(w_used, BR0 + 2 * n + 2)
                dve.wait_ge(sig_ready, 2 * n + 2)
                step(nc.vector.tensor_tensor(gated_b[:, jj, :], bank[4 * n + 2 + jj][:, :],
                                             flat(gateT[:, 8 + 2 * j:10 + 2 * j, :]), ALU.mult))
                nc.vector.tensor_tensor(gated_a[:, jj, :], gated_a[:, jj, :], gated_b[:, jj, :], ALU.add)\
                    .then_inc(mixed, 1)
                dve.wait_ge(mix_hi, j + 1)
                low(flat(mixT_lo[:, 2 * j:2 * j + 2, :]), gated_a[:, jj, :], flat(mixT_hi[:, 2 * j:2 * j + 2, :]))\
                    .then_inc(mix_lo, 1)
                if j == 1:
                    split(25)
                    split(26)
            for c in range(27, 32):
                split(c)

            def wait_tile(t, c, n, used):
                i = 2 * t + c
                dve.wait_ge(*((tile_done, 3 * n + i + 1) if i < 3 else (w_used, used)))

            def add_residual(n, used, banks, done):
                for t in range(TOK):
                    for c in range(2):
                        wait_tile(t, c, n, used)
                        s = res[:, t, 512 * c:512 * c + 512]
                        last = nc.vector.tensor_tensor(s, bank[banks[2 * t + c]][:, :], s, ALU.add)
                    last.then_inc(done, 1)

            add_residual(0, OUT0 + 4, (0, 1, 2, 3), x1_ready)
            dve.wait_ge(x1_ready, TOK)
            for t in range(TOK):
                last = sum_squares(xs[:, t, :], res[:, t, :], X1, t)
            last.then_inc(sumsq_dve, 1)
            split(32)
            for k in range(KT):
                low_T(X1, k, hT_hi, hT_lo, G_CROSS)
            split(33)
            dve.wait_ge(rstd_ready, 3)
            step(nc.vector.tensor_scalar(x_scale[:, :], rstd[:, X1, :], XDH ** -0.5, None, ALU.mult))
            for h in range(XH):
                dve.wait_ge(x_s, h + 1)
                step(nc.vector.tensor_reduce(x_max[:, h, :], bank[h][:, :].rearrange("p (t k) -> p t k", t=TOK),
                                             axis=AX, op=ALU.max))
                nc.vector.scalar_tensor_tensor(x_bias[:, h, :], x_max[:, h, :], -1.0, x_scale[:, :], ALU.mult,
                                               ALU.mult).then_inc(x_biased, 1)
            split(34)
            for h in range(XH):
                dve.wait_ge(x_exp, h + 1)
                step(nc.vector.reciprocal(x_rsum[:, h, :], x_sum[:, h, :]))
                for t in range(TOK):
                    s = x_p[:, h, SEQ * t:SEQ * t + SEQ]
                    last = nc.vector.tensor_scalar(s, s, x_rsum[:, h, t:t + 1], None, ALU.mult)
                last.then_inc(x_normed, 1)
            for h in range(XH):
                dve.wait_ge(x_t, h + 1)
                nc.vector.tensor_copy(x_pT[:, h, :], bank[(7, 4)[h % 2]][:, :]).then_inc(x_pt, 1)
            split(35)
            for p in range(2):
                dve.wait_ge(xo_hi, p + 1)
                low(flat(aT_lo[:, 2 * p:2 * p + 2, :]), bank[p][:, :], flat(aT_hi[:, 2 * p:2 * p + 2, :]))\
                    .then_inc(xo_lo, 1)
            split(36)
            split(37)
            add_residual(1, XO0 + 2, (2, 3, 5, 6), x2_ready)
            split(38)
            for k in range(KT):
                low_T(X2, k, hT_hi, hT_lo, G_MLP)
            split(39)
            for t in range(TOK):
                last = sum_squares(xs[:, t, :], res[:, t, :], X2, t)
            step(last)
            step(nc.vector.tensor_scalar(var[:, X2, :], stat[:, X2, :], 1.0 / D, EPS, ALU.mult, ALU.add))
            step(nc.vector.reciprocal(rstd[:, X2, :], var[:, X2, :]))

            def square_low(b, n):
                dve.wait_ge(u_relu, n)
                nc.vector.tensor_tensor(relu2[:, b, :], relu[:, b, :], relu[:, b, :], ALU.mult).then_inc(u_sq, 1)
                dve.wait_ge(u_sq, n)
                dve.wait_ge(u_hi, n)
                low(flat(aT_lo[:, 4 + 2 * b:6 + 2 * b, :]), relu2[:, b, :], flat(aT_hi[:, 4 + 2 * b:6 + 2 * b, :]))\
                    .then_inc(u_lo, 1)

            square_low(0, 1)
            square_low(1, 2)
            with dve.Fori(0, ITERS) as i:
                for j in range(2):
                    for s in (2 * j + 1, 2 * j + 2):
                        c = LOOP0 + s
                        split_lo(c % RING, c % RAW, 4 * i + (c + 1))
                    square_low(j, 2 * i + (j + 3))
            def x3(t, c):
                wait_tile(t, c, 2, LAST + 1)
                s = res[:, t, 512 * c:512 * c + 512]
                nc.vector.scalar_tensor_tensor(s, bank[(2, 3, 5, 6)[2 * t + c]][:, :], rstd[:, X2, t:t + 1], s,
                                               ALU.mult, ALU.add).then_inc(x3_ready, 1)

            def gain(t):
                dve.wait_ge(x3_ready, TOK * (t + 1))
                step(nc.vector.tensor_tensor(xs[:, t, :], res[:, t, :], gfin[:, :], ALU.mult))

            def normed(t):
                dve.wait_ge(rstd_ready, 4 + t)
                nc.vector.tensor_scalar(xs[:, t, :], xs[:, t, :], rstd[:, X3, t:t + 1], None, ALU.mult)\
                    .then_inc(fin, 1)

            x3(0, 0)
            x3(0, 1)
            dve.wait_ge(gfin_in, 16)
            gain(0)
            x3(1, 0)
            x3(1, 1)
            normed(0)
            gain(1)
            normed(1)

        @block.tensor
        def _(pe):
            mm, tr = nc.tensor.matmul, nc.tensor.transpose

            def weights_T(slot, xh, xl, k0, nk, outs, used, kt_wait=None):
                cols = CH // nk
                if used is not None:
                    pe.wait_ge(w_lo_ready, used)
                order = [(k, m) for m in range(len(outs)) for k in range(nk)]
                if kt_wait:
                    order = [(k, m) for k in range(nk) for m in range(len(outs))]
                for k, m in order:
                    if kt_wait and m == 0:
                        kt_wait(k)
                    at_ = k * cols + m * P
                    wh, wl = w_hi[:, slot, at_:at_ + P], w_lo[:, slot, at_:at_ + P]
                    first = k == 0 and (m == 0 or not kt_wait)
                    for n, (w, v) in enumerate(((wh, xh), (wh, xl), (wl, xh))):
                        last = mm(outs[m], w, v[:, k0 + k, :], start=first and n == 0, stop=k == nk - 1 and n == 2,
                                  skip_group_check=bool(kt_wait))
                last.then_inc(w_used, 1)

            def weights_move(slot, xh, xl, k0, nk, outs, used, start, stop, tiles=False):
                cols = CH // nk
                pe.wait_ge(w_lo_ready, used)
                for t in range(TOK):
                    for cs in ([[0], [1]] if tiles else [range(cols // 512)]):
                        for k in range(nk):
                            sh, sl = xh[:, k0 + k, t * P:(t + 1) * P], xl[:, k0 + k, t * P:(t + 1) * P]
                            for n, (s, w) in enumerate(((sh, w_hi), (sh, w_lo), (sl, w_hi))):
                                for c in cs:
                                    last = mm(outs[t][c], s, w[:, slot, k * cols + 512 * c:k * cols + 512 * c + 512],
                                              start=start and k == 0 and n == 0, stop=stop and k == nk - 1 and n == 2)
                        if tiles and (t, cs) != (TOK - 1, [1]):
                            last.then_inc(tile_done, 1)
                last.then_inc(w_used, 1)

            def halves(b):
                return [bank[b][:, 0:SEQ], bank[b][:, SEQ:2 * SEQ]]

            def transpose_stream(n, src, before=None):
                for k in range(KT):
                    if before:
                        before(k)
                    for t in range(TOK):
                        last = tr(t_tile(n, k)[:, t * P:(t + 1) * P], src[:, t, k * P:(k + 1) * P], ident[:, :])
                    last.then_inc(transposed[n], 1)

            pe.wait_ge(ident_ready, 1)
            pe.wait_ge(g_mix_in, 16)
            tr(bank[7][:, 256:264], g_mix_rows[:, :], ident[0:8, 0:8]).then_inc(gT_done, 1)
            for t in range(TOK):
                pe.wait_ge(x_in[t], 16)
                for k in range(KT):
                    if k == KT - 1 and t == 0:
                        pe.wait_ge(gT_ready, 1)
                    last = tr(t_tile(X, k)[:, t * P:(t + 1) * P], res[:, t, k * P:(k + 1) * P], ident[:, :])
                    if t == TOK - 1:
                        last.then_inc(transposed[X], 1)

            def first_tiles(k):
                pe.wait_ge(lo_done[X], k + 1)
                if k == KT // 2:
                    pe.wait_ge(w_lo_ready, 1)

            for j in range(4):
                pe.wait_ge(*((first_lo, 1) if j == 0 else (w_lo_ready, j + 1)))
                weights_T(j, hT_hi, hT_lo, 0, KT, halves(j), None, first_tiles if j == 0 else None)
                if j == 0:
                    pe.wait_ge(diag_ready, 1)
                    pe.wait_ge(masks_ready, 1)
                    mm(bank[6][:, 0:SEQ], neg_ones[:, :], rstd_diag[:, :], start=True, stop=True).then_inc(row_done, 1)
            for j in range(4):
                pe.wait_ge(qk_evac, j + 1)
                weights_T(j, hT_hi, hT_lo, 0, KT, halves(j), 4 + j + 1)
            pe.wait_ge(g_in, 48)
            pe.wait_ge(lo_done[X], KT)
            tr(bank[4][:, 0:24], g_rows[:, :], ident[0:24, 0:24]).then_inc(gT_done, 1)

            for b in range(2):
                pe.wait_ge(qk_evac, 4 + 2 * b + 2)
                for j in range(2):
                    c = 8 + 2 * b + j
                    weights_move(c % RING, hT_hi, hT_lo, 4 * j, 4, [[bank[2 * b]], [bank[2 * b + 1]]], c + 1,
                                 j == 0, j == 1)
                    if c == 8:
                        pe.wait_ge(mem_scaled, TOK)
                        transpose_stream(MEM, mem_tok, lambda k: pe.wait_ge(gT_ready, 2) if k == 0 else None)

            def scores(h):
                r = slice(DH * (h % 2), DH * (h % 2) + DH)
                q, k = qkT[r, h // 2, :], qkT[r, 4 + h // 2, :]
                s = bank[MO_S]
                if h:
                    pe.wait_ge(mo_biased, h)
                mm(s[:, 0:128], q[:, 0:P], k[:, 0:P], start=True, stop=True)
                mm(s[:, 128:384], q[:, P:SEQ], k, start=True, stop=True).then_inc(mo_s, 1)
                q, k = qkT[r, 8 + h // 2, :], qkT[r, 12 + h // 2, :]
                z = bank[SB_Z[h % 2]]
                if h >= 2:
                    pe.wait_ge(sb_exp, h - 1)
                mm(z[:, 0:256], k[:, 0:P], q, start=True, stop=False, skip_group_check=True)
                mm(z[:, 256:384], k[:, P:SEQ], q[:, P:SEQ], start=False, stop=False, skip_group_check=True)
                if h == 0:
                    pe.wait_ge(masks_ready, 2)
                mm(z[:, 0:384].rearrange("p (b q) -> p b q", b=3)[:, 0:3:2, :], ident_r[:, :], future_r[:, :, :],
                   start=False, stop=False, skip_group_check=True).then_inc(sb_z, 1)

            pe.wait_ge(lo_done[MEM], KT)
            pe.wait_ge(v_evac, 4)
            scores(0)
            for h in range(HEADS):
                c = GATE0 + h
                if h >= 2:
                    pe.wait_ge(gate_evac, h - 1)
                pe.wait_ge(w_lo_ready, c + 1)
                for m in range(2):
                    for kk in range(KT):
                        a = kk * 256 + m * P
                        wh, wl = w_hi[:, c % RING, a:a + P], w_lo[:, c % RING, a:a + P]
                        for n, (w, v) in enumerate(((wh, hT_hi), (wh, hT_lo), (wl, hT_hi))):
                            last = mm(halves(h % 2)[m], w, v[:, kk, :], start=kk == 0 and n == 0,
                                      stop=kk == KT - 1 and n == 2)
                    if m == 0:
                        z, sp_ = bank[SB_Z[h % 2]], sb_sp[:, h % 2, :]
                        pe.wait_ge(sb_raw, h + 1)
                        mm(z[:, 0:256], neg_tri[:, :], sp_[:, 0:256], start=False, stop=False, skip_group_check=True)
                        mm(z[:, 128:256], neg_ones[:, :], sp_[:, 256:384], start=False, stop=False,
                           skip_group_check=True)
                        mm(z[:, 256:384], neg_tri[:, :], sp_[:, 256:384], start=False, stop=True,
                           skip_group_check=True).then_inc(sb_c, 1)
                        pe.wait_ge(mo_normed, h + 1)
                        if h:
                            pe.wait_ge(mo_pt, h)
                        for j in range(3):
                            t = tr(bank[MO_PT][:, P * j:P * j + P], mo_u[:, h % 2, P * j:P * j + P], ident[:, :])
                        t.then_inc(mo_t, 1)
                        if h + 1 < HEADS:
                            scores(h + 1)
                last.then_inc(w_used, 1)

                r = slice(DH * (h % 2), DH * (h % 2) + DH)
                pe.wait_ge(mo_pt, h + 1)
                if h >= 2 and h % 2 == 0:
                    pe.wait_ge(att_lo, h)
                for b, (o, a_, done) in enumerate(((bank[MO_O], mo_pT, mo_av), (bank[SB_O], sb_aT, sb_av))):
                    if b == 1:
                        pe.wait_ge(sb_exp, h + 1)
                    v0 = b * WIDTH + DH * h
                    a_ = a_[:, h % 2, :]
                    mm(o[r, 0:256], v_tok[:, 0, v0:v0 + DH], a_[:, 0:256], start=True, stop=False)
                    mm(o[r, 128:256], v_tok[:, 1, v0:v0 + DH], a_[:, 256:384], start=False, stop=True)\
                        .then_inc(done, 1)

            pe.wait_ge(gate_evac, 8)
            weights_T(MK[0] % RING, mT_hi, mT_lo, 0, KT, halves(0), MK[0] + 1)

            pe.wait_ge(mk_evac, 1)
            pe.wait_ge(att_lo, 8)
            for n in range(2):
                for b in range(2):
                    c = BR0 + 2 * n + b
                    o = 4 * n + 2 * b
                    if c == BR0 + 1:
                        pe.wait_ge(mo_pt, HEADS)
                    if c == BR0 + 2:
                        pe.wait_ge(sb_exp, HEADS)
                    weights_T(c % RING, aT_hi, aT_lo, 4 * b, 4, halves(o) + halves(o + 1), c + 1)

            for j in range(4):
                c = OUT0 + j
                pe.wait_ge(mix_lo, j + 1)
                if j == 0:
                    pe.wait_ge(mixed, 2)
                weights_move(c % RING, mixT_hi, mixT_lo, 2 * j, 2, [[bank[0], bank[1]], [bank[2], bank[3]]], c + 1,
                             j == 0, j == 3, tiles=j == 3)

            pe.wait_ge(mix_lo, 4)
            weights_T(MK[1] % RING, mT_hi, mT_lo, 0, KT, halves(4), MK[1] + 1)
            pe.wait_ge(x1_ready, TOK)
            transpose_stream(X1, res)
            mv_out = [[bank[5]], [bank[6]]]
            weights_move(MV[0] % RING, mT_hi, mT_lo, 0, 4, mv_out, MV[0] + 1, True, False)

            pe.wait_ge(lo_done[X1], KT)
            pe.wait_ge(mk_evac, 2)
            for j in range(2):
                weights_T((XQ0 + j) % RING, hT_hi, hT_lo, 0, KT, halves((7, 4)[j]), XQ0 + j + 1)
            for h in range(XH):
                pe.wait_ge(xq_evac, h // 2 + 1)
                for t in range(TOK):
                    last = mm(bank[h][:, SEQ * t:SEQ * t + SEQ], xqT[:, h, t * P:(t + 1) * P], mkT[:, h, :],
                              start=True, stop=True)
                last.then_inc(x_s, 1)
            weights_move(MV[1] % RING, mT_hi, mT_lo, 4, 4, mv_out, MV[1] + 1, False, True)
            for h in range(XH):
                pe.wait_ge(x_normed, h + 1)
                if h >= 2:
                    pe.wait_ge(x_pt, h - 1)
                b_ = bank[(7, 4)[h % 2]]
                for kt in range(2):
                    for t in range(TOK):
                        last = tr(b_[:, SEQ * kt + P * t:SEQ * kt + P * t + P],
                                  x_p[:, h, SEQ * t + P * kt:SEQ * t + P * kt + P], ident[:, :])
                last.then_inc(x_t, 1)
            pe.wait_ge(mv_evac, TOK)
            for h in range(XH):
                pe.wait_ge(x_pt, h + 1)
                for kt in range(2):
                    last = mm(bank[h // 2][:, SEQ * (h % 2):SEQ * (h % 2) + SEQ], mv_tok[:, kt, XDH * h:XDH * h + XDH],
                              x_pT[:, h, SEQ * kt:SEQ * kt + SEQ], start=kt == 0, stop=kt == 1)
                last.then_inc(x_av, 1)

            acc = [[bank[2], bank[3]], [bank[5], bank[6]]]
            for j in range(2):
                pe.wait_ge(xo_lo, j + 1)
                weights_move((XO0 + j) % RING, aT_hi, aT_lo, 2 * j, 2, acc, XO0 + j + 1, j == 0, j == 1, tiles=j == 1)
            pe.wait_ge(x2_ready, TOK)
            transpose_stream(X2, res)

            def up(b, slot, used, relus, kt_wait=None):
                if relus is not None:
                    pe.wait_ge(u_relu, relus)
                weights_T(slot, hT_hi, hT_lo, 0, KT, halves(b), used, kt_wait)

            def down(b, slot, used, lows, start=False, stop=False):
                pe.wait_ge(u_lo, lows)
                weights_move(slot, aT_hi, aT_lo, 4 + 2 * b, 2, acc, used, start, stop, tiles=stop)

            up(0, UP0 % RING, UP0 + 1, None, lambda k: pe.wait_ge(lo_done[X2], max(k + 1, 2)))
            up(1, (UP0 + 1) % RING, UP0 + 2, None)
            down(0, (UP0 + 2) % RING, UP0 + 3, 1, start=True)
            with pe.Fori(0, ITERS) as i:
                for j in range(2):
                    c = LOOP0 + 2 * j
                    up(j, c % RING, 4 * i + (c + 1), 2 * i + (j + 1))
                    down(1 - j, (c + 1) % RING, 4 * i + (c + 2), 2 * i + (j + 2))
            down((PAIRS - 1) % 2, LAST % RING, LAST + 1, PAIRS, stop=True)


_INS = ['x', 'mem', 'g_mix', 'w_in', 'w_br_moba', 'w_br_sb', 'w_out', 'g_cross', 'g_mem', 'w_xq', 'w_xkv', 'w_xo',
        'g_mlp', 'w_up', 'w_down', 'g_final']


def kernel(**inputs):
    import numpy as np
    import concourse.bacc as bacc
    from concourse.bass_utils import run_bass_kernel_spmd

    nc = bacc.Bacc("TRN2", target_bir_lowering=False, num_devices=1)
    arrays, args = {}, []
    for name in _INS:
        a = np.ascontiguousarray(inputs[name])
        arrays[f"in_{name}_dram"] = a
        args.append(nc.dram_tensor(f"in_{name}_dram", a.shape, mybir.dt.from_np(a.dtype), kind="ExternalInput").ap())
    shape = inputs["x"].shape
    args.append(nc.dram_tensor("out_dram", shape, mybir.dt.float32, kind="ExternalOutput").ap())
    hybrid_layer(nc, *args)
    return run_bass_kernel_spmd(nc, [arrays], core_ids=[0]).results[0]["out_dram"]
```

```python
import concourse.bass as bass
from concourse import mybir
from contextlib import ExitStack

P = 128


def weight_chunks(width, xw, d, ff):
    qkv, at = 3 * width, {}
    cols = [("w_in", 0, 8, base + 256 * j, 256) for base in (0, qkv) for j in range(4)]
    cols += [("w_in", 4 * j, 4, base, 512) for base in (2 * width, qkv + 2 * width) for j in range(2)]
    at["gate"] = len(cols)
    cols += [("w_in", 0, 8, 2 * qkv + 256 * j, 256) for j in range(2 * d // 256)]
    mem_k = [("w_xkv", 0, 8, 256 * j, 256) for j in range(2)]
    mem_v = [("w_xkv", 4 * j, 4, xw, 512) for j in range(2)]
    at["mem_k0"] = len(cols)
    cols += [mem_k[0]]
    at["branch"] = len(cols)
    cols += [(w, 0, 4, 512 * n, 512) for n in range(2) for w in ("w_br_moba", "w_br_sb")]
    at["out"] = len(cols)
    cols += [("w_out", 2 * j, 2, 0, 1024) for j in range(4)]
    at["mem_k1"], at["mem_v0"], at["xq"], at["mem_v1"] = (len(cols) + j for j in (0, 1, 2, 4))
    cols += [mem_k[1], mem_v[0]] + [("w_xq", 0, 8, 256 * j, 256) for j in range(2)] + [mem_v[1]]
    at["xo"] = len(cols)
    cols += [("w_xo", 2 * j, 2, 0, 1024) for j in range(2)]
    at["up"] = len(cols)
    pairs = ff // 256
    up = [("w_up", 0, 8, 256 * i, 256) for i in range(pairs)]
    down = [("w_down", 2 * i, 2, 0, d) for i in range(pairs)]
    cols += [up[0]]
    for i in range(1, pairs):
        cols += [up[i], down[i - 1]]
    cols += [down[-1]]
    return cols, at


def hybrid_layer(nc, x, xT, mem, memT, gains, g_final, weights, ff, out):
    fp32, f32r = mybir.dt.float32, mybir.dt.float32r
    ACT, ALU = mybir.ActivationFunctionType, mybir.AluOpType
    AX = mybir.AxisListType.X

    SEQ, D = x.shape[1], x.shape[2]
    TOK = SEQ // P
    KT = D // P
    HEADS, DH = 8, 64
    WIDTH = HEADS * DH
    XH, XDH = 4, 128
    XW = XH * XDH
    RING, RAW = 4, 6
    CH = 2048
    PAIRS = ff // (2 * P)
    EPS, NEG = 1e-6, -1e30
    assert (SEQ, TOK, KT) == (256, 2, 8)

    chunks, at_chunk = weight_chunks(WIDTH, XW, D, ff)
    GATE0, BR0, OUT0, XQ0, XO0, UP0 = (at_chunk[n] for n in ("gate", "branch", "out", "xq", "xo", "up"))
    MK = [at_chunk["mem_k0"], at_chunk["mem_k1"]]
    MV = [at_chunk["mem_v0"], at_chunk["mem_v1"]]
    LOOP0 = UP0 + 3
    assert (GATE0, BR0, OUT0, XQ0, XO0, UP0) == (12, 21, 25, 31, 34, 36)
    LAST = len(chunks) - 1
    BODY = 12
    PEEL = (LAST - LOOP0) % BODY
    LOOP0 += PEEL
    ITERS = (LAST - LOOP0) // BODY
    assert (BODY % RING, BODY % RAW, PEEL % 4) == (0, 0, 0) and LAST == UP0 + 2 * PAIRS - 1
    X_PIECES = [(0, 1), (1, 2), (2, 4), (4, 6), (6, 8)]
    PIECES = [(0, *p) for p in X_PIECES] + [(1, k, k + 2) for k in range(0, 8, 2)] + [(2, 0, 4), (2, 4, 8)]

    def piece_no(i):
        return sum(k1 < KT for _, _, k1 in PIECES[:i + 1])

    ctx = ExitStack()
    with ctx:
        at = [(nc.sbuf_base + 31) // 32 * 32]

        def place(name, shape, dt=fp32, over=None):
            size = 4
            for s in shape[1:]:
                size *= s
            offset = at[0] if over is None else over
            t = nc.alloc_sbuf_tensor_at(name, shape, dt, offset=offset)
            if over is None:
                at[0] += (size + 31) // 32 * 32
            return t, offset

        def sb(name, shape, dt=fp32, over=None):
            return place(name, shape, dt, over)[0]

        def sem(name):
            return ctx.enter_context(nc.semaphore(name))

        raw, o = place("raw", [P, RAW, CH])
        w_lo = sb("w_lo", [P, RAW, CH], f32r, over=o)
        w_hi = sb("w_hi", [P, RING, CH], f32r)
        res = sb("res", [P, TOK, D])
        hT_hi = sb("hT_hi", [P, KT, SEQ], f32r)
        hT_lo = sb("hT_lo", [P, KT, SEQ], f32r)
        mT_hi = sb("mT_hi", [P, KT, SEQ], f32r)
        mT_lo = sb("mT_lo", [P, KT, SEQ], f32r)
        qkT, o = place("qkT", [P, 16, SEQ])
        zeros = sb("zeros", [P, P], over=o)
        xT_raw = sb("xT_raw", [P, KT, SEQ], over=o + 8192)
        mixT_hi = sb("mixT_hi", [P, KT, SEQ], f32r, over=o)
        mixT_lo = sb("mixT_lo", [P, KT, SEQ], f32r, over=o + 8192)
        xqT = sb("xqT", [P, XH, SEQ], over=o)
        v_tok, o = place("v_tok", [P, TOK, 2 * WIDTH])
        mkT = sb("mkT", [P, XH, SEQ], over=o)
        mv_tok = sb("mv_tok", [P, TOK, XW], over=o + 4096)
        gfin = sb("gfin", [P, D], over=o)
        gateT, o = place("gateT", [P, 16, SEQ])
        xs = sb("xs", [P, TOK, D], over=o)
        memT_raw = sb("memT_raw", [P, KT, SEQ], over=o)
        mem_tok = sb("mem_tok", [P, TOK, D], over=o + 8192)
        aT_hi = sb("aT_hi", [P, 8, SEQ], f32r)
        aT_lo = sb("aT_lo", [P, 8, SEQ], f32r)
        alibi, o = place("alibi", [P, HEADS, SEQ])
        mo_u = sb("mo_u", [P, 2, 384])
        mo_pT = sb("mo_pT", [P, 2, 384])
        sb_aT = sb("sb_aT", [P, 2, 384])
        sb_t = sb("sb_t", [P, 384])
        sb_sp = sb("sb_sp", [P, 384])
        sp_hi = sb("sp_hi", [P, 384], f32r)
        sp_lo = sb("sp_lo", [P, 384], f32r)
        gated_a = sb("gated_a", [P, 2, 512], over=o)
        gated_b = sb("gated_b", [P, 2, 512], over=o + 4096)
        x_p = sb("x_p", [P, XH, 512], over=o)
        x_pT = sb("x_pT", [P, XH, 512], over=o + 8192)
        relu = sb("relu", [P, 2, 512], over=o)
        relu2 = sb("relu2", [P, 2, 512], over=o + 4096)
        ident = sb("ident", [P, P])
        neg_ones = sb("neg_ones", [P, P])
        ident_r = sb("ident_r", [P, P], f32r)
        neg_tri_r = sb("neg_tri_r", [P, P], f32r)
        future_r = sb("future_r", [P, 2, P], f32r)
        gT = sb("gT", [P, 32])
        rstd_diag = sb("rstd_diag", [P, SEQ])
        rstd_row = sb("rstd_row", [P, 2, SEQ])
        mem_row = sb("mem_row", [P, 2, SEQ])
        half = sb("half", [P, 2])
        stat = sb("stat", [P, 5, 2])
        var = sb("var", [P, 5, 2])
        rstd = sb("rstd", [P, 5, 2])
        mo_max = sb("mo_max", [P, 2])
        mo_nmax = sb("mo_nmax", [P, 2])
        mo_sum = sb("mo_sum", [P, 2])
        mo_rsum = sb("mo_rsum", [P, 2])
        x3_ms = sb("x3_ms", [P, TOK, 2])
        x_scale = sb("x_scale", [P, 2])
        x_max = sb("x_max", [P, XH, 2])
        x_bias = sb("x_bias", [P, XH, 2])
        x_sum = sb("x_sum", [P, XH, 2])
        x_rsum = sb("x_rsum", [P, XH, 2])
        assert at[0] <= nc.sbuf_usable_end
        X, MEM, X1, X2, X3 = range(5)
        G_MIX, G_CROSS, G_MEM, G_MLP = range(0, 32, 8)

        bank = [ctx.enter_context(nc.psum_tensor(f"bank{i}", [P, 512], fp32))[:, :] for i in range(8)]
        MO_S, MO_PT, SB_Z, MO_O, SB_O = 2, 3, (4, 5), 6, 7
        WARM_UP = 8
        V_BANKS, MV_BANKS, X_S, X_PT = ((0, 1), (6, 7)), (5, 2), (0, 1, 3, 6), (7, 4, 3, 6)
        X_ROW_BANK, MEM_ROW_BANK = 7, 3

        x_in = [sem(f"x_in{t}") for t in range(TOK)]
        xT_in = [sem(f"xT_in{q}") for q in range(len(X_PIECES))]
        piece_in = [sem(f"piece_in{i}") for i in range(len(PIECES))]
        piece_hi, piece_lo = sem("piece_hi"), sem("piece_lo")
        diag_ready, row_done, row_ready = sem("diag_ready"), sem("row_done"), sem("row_ready")
        gains_in, memT_in, mem_in, gfin_in = sem("gains_in"), sem("memT_in"), sem("mem_in"), sem("gfin_in")
        raw_in = [sem(f"raw_in{s}") for s in range(RAW)]
        stored = sem("stored")
        ident_ready, masks_ready, alibi_ready = sem("ident_ready"), sem("masks_ready"), sem("alibi_ready")
        zeros_ready = sem("zeros_ready")
        pool_step, dve_step = sem("pool_step"), sem("dve_step")
        w_hi_ready, w_lo_ready, w_used = sem("w_hi_ready"), sem("w_lo_ready"), sem("w_used")
        half_ready, sumsq_act, sumsq_dve = sem("half_ready"), sem("sumsq_act"), sem("sumsq_dve")
        rstd_ready = sem("rstd_ready")
        NAMES = {X: "x", MEM: "mem", X1: "x1", X2: "x2"}
        transposed = {n: sem(f"{NAMES[n]}_transposed") for n in (X1, X2)}
        hi_done = {n: sem(f"{s}_hi_done") for n, s in NAMES.items()}
        lo_done = {n: sem(f"{s}_lo_done") for n, s in NAMES.items()}
        qk_evac, v_evac, gate_evac = sem("qk_evac"), sem("v_evac"), sem("gate_evac")
        mo_s, mo_biased, mo_exp, mo_normed = sem("mo_s"), sem("mo_biased"), sem("mo_exp"), sem("mo_normed")
        mo_t, mo_pt, mo_av = sem("mo_t"), sem("mo_pt"), sem("mo_av")
        sb_z, sb_abs, sb_e, sb_ln = sem("sb_z"), sem("sb_abs"), sem("sb_e"), sem("sb_ln")
        sb_raw, sp_hi_done, sp_lo_done, sb_c = sem("sb_raw"), sem("sp_hi_done"), sem("sp_lo_done"), sem("sb_c")
        sb_exp, sb_av = sem("sb_exp"), sem("sb_av")
        att_hi, att_lo = sem("att_hi"), sem("att_lo")
        sig_ready = sem("sig_ready")
        mixed, mix_hi, mix_lo = sem("mixed"), sem("mix_hi"), sem("mix_lo")
        x1_ready, x2_ready = sem("x1_ready"), sem("x2_ready")
        mk_evac, mv_evac, xq_evac = sem("mk_evac"), sem("mv_evac"), sem("xq_evac")
        x_s, x_biased, x_exp, x_normed = sem("x_s"), sem("x_biased"), sem("x_exp"), sem("x_normed")
        x_t, x_pt, x_av, xo_hi, xo_lo = sem("x_t"), sem("x_pt"), sem("x_av"), sem("xo_hi"), sem("xo_lo")
        u_relu, u_sq, u_hi, u_lo = sem("u_relu"), sem("u_sq"), sem("u_hi"), sem("u_lo")
        tile_done, x3_ready, gained = sem("tile_done"), sem("x3_ready"), sem("gained")
        fin, fin_act = sem("fin"), sem("fin_act")

        block = ctx.enter_context(nc.Block())

        @block.sync
        def _(sp):
            def load(c, slot, used=None):
                if used is not None:
                    sp.wait_ge(w_used, used)
                sp.dma_start(raw[:, slot, :], weights[bass.ds(c, 1), :, :].rearrange("c p n -> (c p) n"))\
                    .then_inc(raw_in[slot], 16)

            def load_piece(i):
                c, k0, k1 = PIECES[i]
                cols = slice(k0 * 256, k1 * 256)
                sp.dma_start(raw[:, c, cols], weights[c, :, cols]).then_inc(raw_in[c] if k1 == KT else piece_in[i], 16)

            for q, (k0, k1) in enumerate(X_PIECES):
                sp.dma_start(xT_raw[:, k0:k1, :], xT[:, k0:k1, :]).then_inc(xT_in[q], 16)
                load_piece(q)
            for i in range(len(X_PIECES), len(PIECES)):
                load_piece(i)
            load(3, 3)
            for t in range(TOK):
                sp.dma_start(res[:, t, :], x[0, t * P:(t + 1) * P, :]).then_inc(x_in[t], 16)
            for c in range(4, LOOP0):
                load(c, c % RAW, c - RAW + 1 if c >= RAW else None)
                if c == 8:
                    sp.dma_start(mem_tok[:, :, :], mem[0, :, :].rearrange("(t p) d -> p t d", p=P)).then_inc(mem_in, 16)
                if c == 9:
                    sp.wait_ge(sumsq_act, 1)
                    sp.wait_ge(sumsq_dve, 1)
                    sp.dma_start(memT_raw[:, :, :], memT[:, :, :]).then_inc(memT_in, 16)
            with sp.Fori(0, ITERS) as i:
                for c in range(LOOP0, LOOP0 + BODY):
                    load(BODY * i + c, c % RAW, BODY * i + (c - RAW + 1))
            load(LAST, LAST % RAW, LAST - RAW + 1)
            sp.wait_ge(x_av, XH)
            sp.dma_start(gfin[:, :], g_final.rearrange("(a d) -> a d", a=1).to_broadcast([P, D])).then_inc(gfin_in, 16)
            for t in range(TOK):
                sp.wait_ge(fin, t + 1)
                if t == TOK - 1:
                    sp.wait_ge(fin_act, 1)
                sp.dma_start(out[0, t * P:(t + 1) * P, :], xs[:, t, :]).then_inc(stored, 16)
            sp.wait_ge(stored, 16 * TOK)

        @block.gpsimd
        def _(pool):
            steps = [0]

            def step(ins):
                steps[0] += 1
                ins.then_inc(pool_step, 1)
                pool.wait_ge(pool_step, steps[0])

            nc.gpsimd.memset(half[:, :], -0.5).then_inc(half_ready, 1)
            step(nc.gpsimd.memset(ident[:, :], 0.0))
            nc.gpsimd.affine_select(out=ident[:, :], in_=ident[:, :], compare_op=ALU.not_equal, fill=1.0, base=0,
                                    pattern=[[-1, P]], channel_multiplier=1).then_inc(ident_ready, 1)

            def rsqrt(n, t0=0, t1=TOK):
                step(nc.gpsimd.tensor_scalar(var[:, n, t0:t1], stat[:, n, t0:t1], 1.0 / D, EPS, ALU.mult, ALU.add))
                nc.gpsimd.tensor_tensor(rstd[:, n, t0:t1], var[:, n, t0:t1], half[:, t0:t1], ALU.pow)\
                    .then_inc(rstd_ready, 1)

            pool.wait_ge(half_ready, 1)
            pool.wait_ge(sumsq_act, 1)
            pool.wait_ge(sumsq_dve, 1)
            rsqrt(X)
            step(nc.gpsimd.memset(neg_ones[:, :], -1.0))
            nc.gpsimd.affine_select(out=neg_tri_r[:, :], in_=neg_ones[:, :], compare_op=ALU.is_ge, fill=0.0, base=0,
                                    pattern=[[-1, P]], channel_multiplier=1).then_inc(masks_ready, 1)
            step(nc.gpsimd.memset(future_r[:, :, :].bitcast(fp32), 0.0))
            step(nc.gpsimd.affine_select(out=future_r[:, :, :], in_=future_r[:, :, :].bitcast(fp32),
                                         compare_op=ALU.is_gt, fill=NEG, base=0, pattern=[[0, 2], [1, P]],
                                         channel_multiplier=-1))
            nc.gpsimd.tensor_copy(ident_r[:, :], ident[:, :]).then_inc(masks_ready, 1)
            step(nc.gpsimd.iota(alibi[:, 0, :], pattern=[[1, SEQ]], base=-P, channel_multiplier=-1,
                                allow_small_or_imprecise_dtypes=True))
            for h in range(HEADS - 1, -1, -1):
                step(nc.gpsimd.tensor_scalar(alibi[:, h, :], alibi[:, 0, :], 2.0 ** (-8.0 * (h + 1) / HEADS), 0.0,
                                             ALU.mult, ALU.add))
            for h in range(HEADS):
                last = nc.gpsimd.affine_select(out=alibi[:, h, :], in_=alibi[:, h, :], compare_op=ALU.is_ge, fill=NEG,
                                               base=P, pattern=[[-1, SEQ]], channel_multiplier=1)
                last.then_inc(alibi_ready, 1)
            pool.wait_ge(sumsq_dve, 2)
            rsqrt(MEM)

            pool.wait_ge(sumsq_dve, 3)
            rsqrt(X1)
            for t in range(TOK):
                pool.wait_ge(sumsq_act, 2 * t + 3)
                step(nc.gpsimd.tensor_scalar(var[:, X3, t:t + 1], x3_ms[:, t, 0:1], x3_ms[:, t, 1:2], EPS, ALU.add,
                                             ALU.add))
                nc.gpsimd.tensor_tensor(rstd[:, X3, t:t + 1], var[:, X3, t:t + 1], half[:, 0:1], ALU.pow)\
                    .then_inc(rstd_ready, 1)

        T_AT = {X1: [(b, m) for b in (0, 1, 6, 7) for m in range(2)],
                X2: [(0, 0), (1, 0), (7, 0), (4, 0), (2, 0), (2, 1), (3, 0), (3, 1)]}

        def t_tile(n, k):
            b, m = T_AT[n][k]
            return bank[b][:, SEQ * m:SEQ * m + SEQ]

        def bank_full(n, k):
            return 1 + max(j for j in range(KT) if T_AT[n][j][0] == T_AT[n][k][0])

        def flat(t):
            return t.rearrange("p b t -> p (b t)")

        @block.scalar
        def _(act):
            copy = nc.scalar.activation
            nc.scalar.preload_act_table_set("natural_log_exp_and_others")
            act.dma_start(gT[:, :], gains[:, :]).then_inc(gains_in, 16)

            def split_hi(slot, rslot, arrived, used):
                act.wait_ge(raw_in[rslot], arrived)
                if used is not None:
                    act.wait_ge(w_used, used)
                copy(w_hi[:, slot, :], raw[:, rslot, :], ACT.Copy).then_inc(w_hi_ready, 1)

            def split(c):
                split_hi(c % RING, c % RAW, 16 * (c // RAW + 1), c - RING + 1 if c >= RING else None)

            def high_T(n, k, dst, g):
                act.wait_ge(transposed[n], bank_full(n, k))
                copy(dst[:, k, :], t_tile(n, k), ACT.Copy, scale=gT[:, g + k:g + k + 1]).then_inc(hi_done[n], 1)

            def high_in(n, k, dst, whole, g):
                copy(dst[:, k, :], whole[:, k, :], ACT.Copy, scale=gT[:, g + k:g + k + 1])\
                    .then_inc(hi_done[n], 1)

            def split_piece(i):
                c, k0, k1 = PIECES[i]
                cols = slice(k0 * 256, k1 * 256)
                act.wait_ge(raw_in[c] if k1 == KT else piece_in[i], 16)
                copy(w_hi[:, c, cols], raw[:, c, cols], ACT.Copy)\
                    .then_inc(w_hi_ready if k1 == KT else piece_hi, 1)

            act.wait_ge(gains_in, 16)
            for q, (k0, k1) in enumerate(X_PIECES):
                act.wait_ge(xT_in[q], 16)
                for k in range(k0, k1):
                    high_in(X, k, hT_hi, xT_raw, G_MIX)
                split_piece(q)
            for i in range(len(X_PIECES), len(PIECES)):
                split_piece(i)
            split(3)
            act.wait_ge(x_in[0], 16)
            copy(xs[:, 0, :], res[:, 0, :], ACT.Square, accum_out=stat[:, X, 0:1]).then_inc(sumsq_act, 1)
            for c in range(4, 12):
                split(c)
            act.wait_ge(rstd_ready, 1)

            def v_out(b):
                act.wait_ge(w_used, 10 + 2 * b)
                for t in range(TOK):
                    copy(v_tok[:, t, b * WIDTH:(b + 1) * WIDTH], bank[V_BANKS[b][t]][:, :], ACT.Copy,
                         scale=rstd[:, X, t:t + 1]).then_inc(v_evac, 1)

            def att_high(p):
                act.wait_ge(mo_av, 2 * p + 2)
                copy(aT_hi[:, p, :], bank[MO_O][:, 0:SEQ], ACT.Copy).then_inc(att_hi, 1)
                act.wait_ge(sb_av, 2 * p + 2)
                copy(aT_hi[:, 4 + p, :], bank[SB_O][:, 0:SEQ], ACT.Copy).then_inc(att_hi, 1)

            def softplus_exp(h):
                act.wait_ge(sb_z, h + 1)
                if h:
                    act.wait_ge(sb_raw, h)
                copy(sb_t[:, :], bank[SB_Z[h % 2]][:, 0:384], ACT.Abs).then_inc(sb_abs, 1)
                act.wait_ge(sb_abs, h + 1)
                copy(sb_t[:, :], sb_t[:, :], ACT.Exp, scale=-1.0).then_inc(sb_e, 1)
                act.wait_ge(sb_e, h + 1)
                copy(sb_t[:, :], sb_t[:, :], ACT.Ln, bias=1.0).then_inc(sb_ln, 1)
                act.wait_ge(mo_biased, h + 1)
                for q, (a, b) in enumerate(((0, 128), (128, 384))):
                    last = copy(mo_u[:, h % 2, a:b], mo_u[:, h % 2, a:b], ACT.Exp, bias=mo_nmax[:, q:q + 1],
                                accum_out=mo_sum[:, q:q + 1])
                last.then_inc(mo_exp, 1)
                act.wait_ge(sb_raw, h + 1)
                copy(sp_hi[:, :], sb_sp[:, :], ACT.Copy).then_inc(sp_hi_done, 1)

            act.wait_ge(memT_in, 16)
            split(12)
            softplus_exp(0)
            v_out(0)
            split(13)
            for k in range(KT):
                high_in(MEM, k, mT_hi, memT_raw, G_MEM)
                if k == KT // 2:
                    split(14)
            v_out(1)
            split(15)
            for h in range(HEADS):
                act.wait_ge(sb_c, h + 1)
                if h >= 2:
                    act.wait_ge(sb_av, h - 1)
                copy(sb_aT[:, h % 2, :], bank[SB_Z[h % 2]][:, 0:384], ACT.Exp).then_inc(sb_exp, 1)
                if h + 1 < HEADS:
                    softplus_exp(h + 1)
                split(GATE0 + h + 4)
                if h % 2:
                    att_high(h // 2)
            act.wait_ge(gate_evac, 8)
            for n in range(2):
                for b in range(2):
                    s = gateT[:, 8 * b + 4 * n:8 * b + 4 * n + 4, :]
                    copy(s, s, ACT.Sigmoid).then_inc(sig_ready, 1)
                if n == 0:
                    split(24)
            for j in range(4):
                act.wait_ge(mixed, j + 1)
                copy(flat(mixT_hi[:, 2 * j:2 * j + 2, :]), gated_a[:, j % 2, :], ACT.Copy).then_inc(mix_hi, 1)
                if j == 1:
                    split(25)
                    split(26)
                if j == 2:
                    split(27)
            for c in range(28, 31):
                split(c)
            nc.scalar.preload_act_table_set("natural_log_exp_and_others")
            split(31)
            for k in range(KT):
                high_T(X1, k, hT_hi, G_CROSS)
            split(32)
            split(33)
            for j in range(2):
                act.wait_ge(w_used, XQ0 + j + 1)
                copy(flat(xqT[:, 2 * j:2 * j + 2, :]), bank[(7, 4)[j]][:, :], ACT.Copy).then_inc(xq_evac, 1)
                if j == 0:
                    split(34)
            for h in range(XH):
                act.wait_ge(x_biased, h + 1)
                for t in range(TOK):
                    last = copy(x_p[:, h, SEQ * t:SEQ * t + SEQ], bank[X_S[h]][:, SEQ * t:SEQ * t + SEQ], ACT.Exp,
                                bias=x_bias[:, h, t:t + 1], scale=x_scale[:, t:t + 1],
                                accum_out=x_sum[:, h, t:t + 1])
                last.then_inc(x_exp, 1)
            act.wait_ge(w_used, MV[1] + 1)
            act.wait_ge(rstd_ready, 2)
            for t in range(TOK):
                copy(mv_tok[:, t, :], bank[MV_BANKS[t]][:, :], ACT.Copy, scale=rstd[:, MEM, t:t + 1])\
                    .then_inc(mv_evac, 1)
            split(35)
            for p in range(2):
                act.wait_ge(x_av, 2 * p + 2)
                copy(flat(aT_hi[:, 2 * p:2 * p + 2, :]), bank[p][:, :], ACT.Copy).then_inc(xo_hi, 1)
            split(36)
            split(37)
            split(38)
            for k in range(KT):
                high_T(X2, k, hT_hi, G_MLP)
            split(39)

            def square_relu(b, used, relu_free, mine):
                act.wait_ge(w_used, used)
                if relu_free is not None:
                    act.wait_ge(u_sq, relu_free)
                copy(relu[:, b, :], bank[b][:, :], ACT.Relu).then_inc(u_relu, 1)
                act.wait_ge(u_relu, mine)
                copy(flat(aT_hi[:, 4 + 2 * b:6 + 2 * b, :]), relu[:, b, :], ACT.Square).then_inc(u_hi, 1)

            square_relu(0, UP0 + 1, None, 1)
            square_relu(1, UP0 + 2, None, 2)

            def mlp_steps(first, n, i=0):
                for c in range(first, first + n, 2):
                    for d in (c + 1, c + 2):
                        split_hi(d % RING, d % RAW, 16 * (BODY // RAW) * i + 16 * (d // RAW + 1),
                                 BODY * i + (d - RING + 1))
                    u = (c - UP0 + 1) // 2
                    square_relu(u % 2, BODY * i + (c + 1), BODY // 2 * i + (u - 1), BODY // 2 * i + (u + 1))

            mlp_steps(LOOP0 - PEEL, PEEL)
            with act.Fori(0, ITERS) as i:
                mlp_steps(LOOP0, BODY, i)
            for t in range(TOK):
                for c in range(2):
                    act.wait_ge(x3_ready, 2 * t + c + 1)
                    copy((relu, relu2)[t][:, c, :], res[:, t, 512 * c:512 * c + 512], ACT.Square, scale=D ** -0.5,
                         accum_out=x3_ms[:, t, c:c + 1]).then_inc(sumsq_act, 1)
            act.wait_ge(gained, 4)
            act.wait_ge(rstd_ready, 5)
            copy(xs[:, 1, D // 2:D], xs[:, 1, D // 2:D], ACT.Copy, scale=rstd[:, X3, 1:2]).then_inc(fin_act, 1)

        @block.vector
        def _(dve):
            steps = [0]

            def step(ins):
                steps[0] += 1
                ins.then_inc(dve_step, 1)
                dve.wait_ge(dve_step, steps[0])

            sub = ALU.subtract

            def low(dst, whole, high):
                return nc.vector.tensor_tensor(dst, whole, high.bitcast(fp32), sub)

            def split_lo(slot, rslot, hi):
                dve.wait_ge(w_hi_ready, hi)
                low(w_lo[:, rslot, :], raw[:, rslot, :], w_hi[:, slot, :]).then_inc(w_lo_ready, 1)

            def split(c):
                split_lo(c % RING, c % RAW, c + 1)

            def low_T(n, k, hi, lo, g):
                dve.wait_ge(hi_done[n], bank_full(n, k))
                nc.vector.scalar_tensor_tensor(lo[:, k, :], t_tile(n, k), gT[:, g + k:g + k + 1],
                                               hi[:, k, :].bitcast(fp32), ALU.mult, sub).then_inc(lo_done[n], 1)

            def sum_squares(scratch, src, n, t):
                return nc.vector.tensor_tensor_reduce(out=scratch, in0=src, in1=src, scale=1.0, scalar=0.0,
                                                      op0=ALU.mult, op1=ALU.add, accum_out=stat[:, n, t:t + 1])

            def low_in(n, k, hi, lo, whole, g):
                dve.wait_ge(hi_done[n], k + 1)
                nc.vector.scalar_tensor_tensor(lo[:, k, :], whole[:, k, :], gT[:, g + k:g + k + 1],
                                               hi[:, k, :].bitcast(fp32), ALU.mult, sub).then_inc(lo_done[n], 1)

            def split_piece(i):
                c, k0, k1 = PIECES[i]
                cols = slice(k0 * 256, k1 * 256)
                dve.wait_ge(*((w_hi_ready, c + 1) if k1 == KT else (piece_hi, piece_no(i))))
                low(w_lo[:, c, cols], raw[:, c, cols], w_hi[:, c, cols])\
                    .then_inc(w_lo_ready if k1 == KT else piece_lo, 1)

            def diagonal(n, rows):
                dve.wait_ge(rstd_ready, rows)
                for t in range(TOK):
                    last = nc.vector.tensor_scalar(rstd_diag[:, t * P:(t + 1) * P], ident[:, :], rstd[:, n, t:t + 1],
                                                   -1.0, ALU.mult, ALU.mult)
                last.then_inc(diag_ready, 1)

            def spread(dst, b, rows):
                dve.wait_ge(row_done, rows)
                for j in range(2):
                    last = nc.vector.tensor_copy(dst[:, j, :], bank[b][:, 0:SEQ])
                last.then_inc(row_ready, 1)

            nc.vector.memset(zeros[:, :], 0.0).then_inc(zeros_ready, 1)
            dve.wait_ge(gains_in, 16)
            for q, (k0, k1) in enumerate(X_PIECES):
                for k in range(k0, k1):
                    low_in(X, k, hT_hi, hT_lo, xT_raw, G_MIX)
                split_piece(q)
            for i in range(len(X_PIECES), len(PIECES)):
                split_piece(i)
            split(3)
            dve.wait_ge(x_in[1], 16)
            sum_squares(xs[:, 1, :], res[:, 1, :], X, 1).then_inc(sumsq_dve, 1)
            dve.wait_ge(ident_ready, 1)
            diagonal(X, 1)
            split(4)
            spread(rstd_row, X_ROW_BANK, 1)
            dve.wait_ge(row_ready, 1)
            for c in range(8):
                dve.wait_ge(w_used, c + 1)
                nc.vector.scalar_tensor_tensor(flat(qkT[:, 2 * c:2 * c + 2, :]), bank[c][:, :],
                                               DH ** -0.5 if c % 4 < 2 else 1.0, flat(rstd_row[:, :, :]),
                                               ALU.mult, ALU.mult).then_inc(qk_evac, 1)
                split(c + 5)
            dve.wait_ge(mem_in, 16)
            for t in range(TOK):
                last = sum_squares(mem_tok[:, t, :], mem_tok[:, t, :], MEM, t)
            last.then_inc(sumsq_dve, 1)

            def att_low(p):
                for b, o in enumerate((MO_O, SB_O)):
                    dve.wait_ge(att_hi, 2 * p + b + 1)
                    low(aT_lo[:, 4 * b + p, :], bank[o][:, 0:SEQ], aT_hi[:, 4 * b + p, :]).then_inc(att_lo, 1)

            def scores(h):
                dve.wait_ge(mo_s, h + 1)
                if h >= 2:
                    dve.wait_ge(mo_t, h - 1)
                for q, (a, b, c) in enumerate(((0, 128, 128), (128, 384, 0))):
                    last = nc.vector.tensor_tensor_reduce(out=mo_u[:, h % 2, a:b], in0=bank[MO_S][:, a:b],
                                                          in1=alibi[:, h, c:SEQ], scale=1.0, scalar=-3e38,
                                                          op0=ALU.add, op1=ALU.max, accum_out=mo_max[:, q:q + 1])
                step(last)
                nc.vector.tensor_scalar(mo_nmax[:, :], mo_max[:, :], -1.0, None, ALU.mult).then_inc(mo_biased, 1)
                dve.wait_ge(sb_ln, h + 1)
                if h:
                    dve.wait_ge(sb_c, h)
                nc.vector.scalar_tensor_tensor(sb_sp[:, :], bank[SB_Z[h % 2]][:, 0:384], 0.0, sb_t[:, :],
                                               ALU.max, ALU.add).then_inc(sb_raw, 1)
                dve.wait_ge(mo_exp, h + 1)
                step(nc.vector.reciprocal(mo_rsum[:, :], mo_sum[:, :]))
                for q, (a, b) in enumerate(((0, 128), (128, 384))):
                    last = nc.vector.tensor_scalar(mo_u[:, h % 2, a:b], mo_u[:, h % 2, a:b], mo_rsum[:, q:q + 1], None,
                                                   ALU.mult)
                last.then_inc(mo_normed, 1)
                dve.wait_ge(sp_hi_done, h + 1)
                low(sp_lo[:, :], sb_sp[:, :], sp_hi[:, :]).then_inc(sp_lo_done, 1)

            dve.wait_ge(alibi_ready, HEADS)
            scores(0)
            diagonal(MEM, 2)
            split(13)
            spread(mem_row, MEM_ROW_BANK, 2)
            for k in range(KT):
                low_in(MEM, k, mT_hi, mT_lo, memT_raw, G_MEM)
                if k == KT // 2:
                    split(14)
            split(15)
            for h in range(HEADS):
                dve.wait_ge(mo_t, h + 1)
                if h >= 2:
                    dve.wait_ge(mo_av, h - 1)
                nc.vector.tensor_copy(mo_pT[:, h % 2, :], bank[MO_PT][:, 0:384]).then_inc(mo_pt, 1)
                if h + 1 < HEADS:
                    scores(h + 1)
                dve.wait_ge(w_used, GATE0 + h + 1)
                nc.vector.tensor_tensor(flat(gateT[:, 2 * h:2 * h + 2, :]), bank[h % 2][:, :],
                                        flat(rstd_row[:, :, :]), ALU.mult).then_inc(gate_evac, 1)
                split(GATE0 + h + 4)
                if h % 2:
                    att_low(h // 2)
            split(24)

            def mem_k_out(i, b):
                dve.wait_ge(row_ready, 2)
                dve.wait_ge(w_used, MK[i] + 1)
                nc.vector.tensor_tensor(flat(mkT[:, 2 * i:2 * i + 2, :]), bank[b][:, :], flat(mem_row[:, :, :]),
                                        ALU.mult).then_inc(mk_evac, 1)

            mem_k_out(0, 3)
            for j in range(4):
                n, jj = j // 2, j % 2
                dve.wait_ge(w_used, BR0 + 2 * n + 1)
                dve.wait_ge(sig_ready, 2 * n + 1)
                if j >= 2:
                    dve.wait_ge(mix_hi, j - 1)
                nc.vector.tensor_tensor(gated_a[:, jj, :], bank[4 * n + jj][:, :], flat(gateT[:, 2 * j:2 * j + 2, :]),
                                        ALU.mult)
                dve.wait_ge(w_used, BR0 + 2 * n + 2)
                dve.wait_ge(sig_ready, 2 * n + 2)
                step(nc.vector.tensor_tensor(gated_b[:, jj, :], bank[4 * n + 2 + jj][:, :],
                                             flat(gateT[:, 8 + 2 * j:10 + 2 * j, :]), ALU.mult))
                nc.vector.tensor_tensor(gated_a[:, jj, :], gated_a[:, jj, :], gated_b[:, jj, :], ALU.add)\
                    .then_inc(mixed, 1)
                dve.wait_ge(mix_hi, j + 1)
                low(flat(mixT_lo[:, 2 * j:2 * j + 2, :]), gated_a[:, jj, :], flat(mixT_hi[:, 2 * j:2 * j + 2, :]))\
                    .then_inc(mix_lo, 1)
                if j == 1:
                    split(25)
                    split(26)
            for c in range(27, 31):
                split(c)

            def wait_tile(t, c, n, used):
                i = 2 * t + c
                dve.wait_ge(*((tile_done, 3 * n + i + 1) if i < 3 else (w_used, used)))

            def add_residual(n, used, banks, done):
                for t in range(TOK):
                    for c in range(2):
                        wait_tile(t, c, n, used)
                        s = res[:, t, 512 * c:512 * c + 512]
                        last = nc.vector.tensor_tensor(s, bank[banks[2 * t + c]][:, :], s, ALU.add)
                    last.then_inc(done, 1)

            add_residual(0, OUT0 + 4, (0, 1, 2, 3), x1_ready)
            split(31)
            mem_k_out(1, 4)
            for k in range(KT):
                low_T(X1, k, hT_hi, hT_lo, G_CROSS)
            split(32)
            dve.wait_ge(x1_ready, TOK)
            for t in range(TOK):
                last = sum_squares(xs[:, t, :], res[:, t, :], X1, t)
            last.then_inc(sumsq_dve, 1)
            split(33)
            dve.wait_ge(rstd_ready, 3)
            step(nc.vector.tensor_scalar(x_scale[:, :], rstd[:, X1, :], XDH ** -0.5, None, ALU.mult))
            for h in range(XH):
                dve.wait_ge(x_s, h + 1)
                step(nc.vector.tensor_reduce(x_max[:, h, :], bank[X_S[h]][:, :].rearrange("p (t k) -> p t k", t=TOK),
                                             axis=AX, op=ALU.max))
                nc.vector.scalar_tensor_tensor(x_bias[:, h, :], x_max[:, h, :], -1.0, x_scale[:, :], ALU.mult,
                                               ALU.mult).then_inc(x_biased, 1)
                if h == 1:
                    split(34)
            for h in range(XH):
                dve.wait_ge(x_exp, h + 1)
                step(nc.vector.reciprocal(x_rsum[:, h, :], x_sum[:, h, :]))
                for t in range(TOK):
                    s = x_p[:, h, SEQ * t:SEQ * t + SEQ]
                    last = nc.vector.tensor_scalar(s, s, x_rsum[:, h, t:t + 1], None, ALU.mult)
                last.then_inc(x_normed, 1)
            for h in range(XH):
                dve.wait_ge(x_t, h + 1)
                nc.vector.tensor_copy(x_pT[:, h, :], bank[X_PT[h]][:, :]).then_inc(x_pt, 1)
            for p in range(2):
                dve.wait_ge(xo_hi, p + 1)
                low(flat(aT_lo[:, 2 * p:2 * p + 2, :]), bank[p][:, :], flat(aT_hi[:, 2 * p:2 * p + 2, :]))\
                    .then_inc(xo_lo, 1)
            split(35)
            split(36)
            split(37)
            add_residual(1, XO0 + 2, (2, 3, 5, 6), x2_ready)
            for k in range(KT):
                low_T(X2, k, hT_hi, hT_lo, G_MLP)
            split(38)

            def square_low(b, n):
                dve.wait_ge(u_relu, n)
                nc.vector.tensor_tensor(relu2[:, b, :], relu[:, b, :], relu[:, b, :], ALU.mult).then_inc(u_sq, 1)
                dve.wait_ge(u_sq, n)
                dve.wait_ge(u_hi, n)
                low(flat(aT_lo[:, 4 + 2 * b:6 + 2 * b, :]), relu2[:, b, :], flat(aT_hi[:, 4 + 2 * b:6 + 2 * b, :]))\
                    .then_inc(u_lo, 1)

            square_low(0, 1)
            split(39)
            square_low(1, 2)
            for t in range(TOK):
                last = sum_squares(xs[:, t, :], res[:, t, :], X2, t)
            step(last)
            step(nc.vector.tensor_scalar(var[:, X2, :], stat[:, X2, :], 1.0 / D, EPS, ALU.mult, ALU.add))
            step(nc.vector.reciprocal(rstd[:, X2, :], var[:, X2, :]))

            def mlp_steps(first, n, i=0):
                for c in range(first, first + n, 2):
                    for d in (c + 1, c + 2):
                        split_lo(d % RING, d % RAW, BODY * i + (d + 1))
                    u = (c - UP0 + 1) // 2
                    square_low(u % 2, BODY // 2 * i + (u + 1))

            mlp_steps(LOOP0 - PEEL, PEEL)
            with dve.Fori(0, ITERS) as i:
                mlp_steps(LOOP0, BODY, i)
            def x3(t, c):
                wait_tile(t, c, 2, LAST + 1)
                s = res[:, t, 512 * c:512 * c + 512]
                nc.vector.scalar_tensor_tensor(s, bank[(2, 3, 5, 6)[2 * t + c]][:, :], rstd[:, X2, t:t + 1], s,
                                               ALU.mult, ALU.add).then_inc(x3_ready, 1)

            def gain(t, c):
                s = slice(512 * c, 512 * c + 512)
                dve.wait_ge(x3_ready, TOK * t + c + 1)
                nc.vector.tensor_tensor(xs[:, t, s], res[:, t, s], gfin[:, s], ALU.mult).then_inc(gained, 1)

            def normed(t, cols):
                dve.wait_ge(gained, 2 * t + 2)
                dve.wait_ge(rstd_ready, 4 + t)
                nc.vector.tensor_scalar(xs[:, t, cols], xs[:, t, cols], rstd[:, X3, t:t + 1], None, ALU.mult)\
                    .then_inc(fin, 1)

            dve.wait_ge(gfin_in, 16)
            for t in range(TOK):
                for c in range(2):
                    x3(t, c)
                    if (t, c) == (1, 1):
                        normed(0, slice(0, D))
                    gain(t, c)
            normed(1, slice(0, D // 2))

        @block.tensor
        def _(pe):
            mm, tr = nc.tensor.matmul, nc.tensor.transpose

            def weights_T(c, xh, xl, k0, nk, outs, used, kt_wait=None, between=None):
                cols = CH // nk
                if used is not None:
                    pe.wait_ge(w_lo_ready, used)
                order = [(k, m) for m in range(len(outs)) for k in range(nk)]
                if kt_wait:
                    order = [(k, m) for k in range(nk) for m in range(len(outs))]
                for k, m in order:
                    if kt_wait and m == 0:
                        kt_wait(k)
                    if between and (k, m) == (0, 1):
                        between()
                    at_ = k * cols + m * P
                    wh, wl = w_hi[:, c % RING, at_:at_ + P], w_lo[:, c % RAW, at_:at_ + P]
                    first = k == 0 and (m == 0 or not kt_wait)
                    for n, (w, v) in enumerate(((wh, xh), (wh, xl), (wl, xh))):
                        last = mm(outs[m], w, v[:, k0 + k, :], start=first and n == 0, stop=k == nk - 1 and n == 2,
                                  skip_group_check=bool(kt_wait))
                last.then_inc(w_used, 1)

            def weights_move(chunk, xh, xl, k0, nk, outs, used, start, stop, tiles=False, between=None):
                cols = CH // nk
                wh, wl = w_hi[:, chunk % RING, :], w_lo[:, chunk % RAW, :]
                pe.wait_ge(w_lo_ready, used)
                for t in range(TOK):
                    for cs in ([[0], [1]] if tiles else [range(cols // 512)]):
                        for k in range(nk):
                            if between and (t, k) == (0, 1):
                                between()
                            sh, sl = xh[:, k0 + k, t * P:(t + 1) * P], xl[:, k0 + k, t * P:(t + 1) * P]
                            for n, (s, w) in enumerate(((sh, wh), (sh, wl), (sl, wh))):
                                for c in cs:
                                    last = mm(outs[t][c], s, w[:, k * cols + 512 * c:k * cols + 512 * c + 512],
                                              start=start and k == 0 and n == 0, stop=stop and k == nk - 1 and n == 2)
                        if tiles and (t, cs) != (TOK - 1, [1]):
                            last.then_inc(tile_done, 1)
                last.then_inc(w_used, 1)

            def halves(b):
                return [bank[b][:, 0:SEQ], bank[b][:, SEQ:2 * SEQ]]

            def transpose_stream(n, src, ready):
                for t in range(TOK):
                    pe.wait_ge(ready, t + 1)
                    for k in range(KT):
                        last = tr(t_tile(n, k)[:, t * P:(t + 1) * P], src[:, t, k * P:(k + 1) * P], ident[:, :])
                        if t == TOK - 1:
                            last.then_inc(transposed[n], 1)

            pe.wait_ge(zeros_ready, 1)
            for _ in range(WARM_UP):
                mm(bank[7][:, 0:P], zeros[:, :], zeros[:, :], start=True, stop=True)

            def pieces_of(c):
                def wait(k):
                    if c == 0:
                        pe.wait_ge(lo_done[X], k + 1)
                    for i, (chunk, k0, k1) in enumerate(PIECES):
                        if (chunk, k0) == (c, k):
                            pe.wait_ge(*((w_lo_ready, c + 1) if k1 == KT else (piece_lo, piece_no(i))))
                return wait

            def spread_rstd(b, n):
                pe.wait_ge(masks_ready, 1)
                pe.wait_ge(diag_ready, n)
                mm(bank[b][:, 0:SEQ], neg_ones[:, :], rstd_diag[:, :], start=True, stop=True).then_inc(row_done, 1)

            for c in range(8):
                if c == X_ROW_BANK:
                    pe.wait_ge(row_ready, 1)
                weights_T(c, hT_hi, hT_lo, 0, KT, halves(c), c + 1 if c > 2 else None,
                          pieces_of(c) if c <= 2 else None,
                          (lambda: spread_rstd(X_ROW_BANK, 1)) if c == 3 else None)

            def scores(h):
                r = slice(DH * (h % 2), DH * (h % 2) + DH)
                q, k = qkT[r, h // 2, :], qkT[r, 4 + h // 2, :]
                s = bank[MO_S]
                if h:
                    pe.wait_ge(mo_biased, h)
                mm(s[:, 0:128], q[:, 0:P], k[:, 0:P], start=True, stop=True)
                mm(s[:, 128:384], q[:, P:SEQ], k, start=True, stop=True).then_inc(mo_s, 1)
                q, k = qkT[r, 8 + h // 2, :], qkT[r, 12 + h // 2, :]
                z = bank[SB_Z[h % 2]]
                if h >= 2:
                    pe.wait_ge(sb_exp, h - 1)
                mm(z[:, 0:256], k[:, 0:P], q, start=True, stop=False, skip_group_check=True)
                mm(z[:, 256:384], k[:, P:SEQ], q[:, P:SEQ], start=False, stop=False, skip_group_check=True)
                if h == 0:
                    pe.wait_ge(masks_ready, 2)
                mm(z[:, 0:384].rearrange("p (b q) -> p b q", b=3)[:, 0:3:2, :], ident_r[:, :], future_r[:, :, :],
                   start=False, stop=False, skip_group_check=True).then_inc(sb_z, 1)

            for c in range(8, 12):
                b, j = divmod(c - 8, 2)
                if c == 8:
                    pe.wait_ge(qk_evac, 2)
                weights_move(c, hT_hi, hT_lo, 4 * j, 4, [[bank[V_BANKS[b][t]]] for t in range(TOK)], c + 1,
                             j == 0, j == 1)
                if c == 9:
                    pe.wait_ge(qk_evac, 8)
                    scores(0)
                if c == 10:
                    spread_rstd(MEM_ROW_BANK, 2)

            for h in range(HEADS):
                c = GATE0 + h
                if h == 0:
                    pe.wait_ge(v_evac, 2)
                if h >= 2:
                    pe.wait_ge(gate_evac, h - 1)
                pe.wait_ge(w_lo_ready, c + 1)
                for m in range(2):
                    for kk in range(KT):
                        a = kk * 256 + m * P
                        wh, wl = w_hi[:, c % RING, a:a + P], w_lo[:, c % RAW, a:a + P]
                        for n, (w, v) in enumerate(((wh, hT_hi), (wh, hT_lo), (wl, hT_hi))):
                            last = mm(halves(h % 2)[m], w, v[:, kk, :], start=kk == 0 and n == 0,
                                      stop=kk == KT - 1 and n == 2)
                    if m == 0:
                        z = bank[SB_Z[h % 2]]
                        pe.wait_ge(sb_raw, h + 1)
                        mm(z[:, 128:256], neg_ones[:, :], sb_sp[:, 256:384], start=False, stop=False,
                           skip_group_check=True)
                        pe.wait_ge(sp_lo_done, h + 1)
                        mm(z[:, 0:384], neg_tri_r[:, :], sp_hi[:, :], start=False, stop=False, skip_group_check=True)
                        mm(z[:, 0:384], neg_tri_r[:, :], sp_lo[:, :], start=False, stop=True,
                           skip_group_check=True).then_inc(sb_c, 1)
                        pe.wait_ge(mo_normed, h + 1)
                        if h:
                            pe.wait_ge(mo_pt, h)
                        else:
                            pe.wait_ge(row_ready, 2)
                        for j in range(3):
                            t = tr(bank[MO_PT][:, P * j:P * j + P], mo_u[:, h % 2, P * j:P * j + P], ident[:, :])
                        t.then_inc(mo_t, 1)
                        if h + 1 < HEADS:
                            scores(h + 1)
                last.then_inc(w_used, 1)

                r = slice(DH * (h % 2), DH * (h % 2) + DH)
                pe.wait_ge(mo_pt, h + 1)
                if h == 0:
                    pe.wait_ge(v_evac, 4)
                if h >= 2 and h % 2 == 0:
                    pe.wait_ge(att_lo, h)
                for b, (o, a_, done) in enumerate(((bank[MO_O], mo_pT, mo_av), (bank[SB_O], sb_aT, sb_av))):
                    if b == 1:
                        pe.wait_ge(sb_exp, h + 1)
                    v0 = b * WIDTH + DH * h
                    a_ = a_[:, h % 2, :]
                    mm(o[r, 0:256], v_tok[:, 0, v0:v0 + DH], a_[:, 0:256], start=True, stop=False)
                    mm(o[r, 128:256], v_tok[:, 1, v0:v0 + DH], a_[:, 256:384], start=False, stop=True)\
                        .then_inc(done, 1)

            pe.wait_ge(lo_done[MEM], KT)
            weights_T(MK[0], mT_hi, mT_lo, 0, KT, halves(3), MK[0] + 1)

            pe.wait_ge(gate_evac, 8)
            pe.wait_ge(att_lo, 8)
            for n in range(2):
                for b in range(2):
                    c = BR0 + 2 * n + b
                    o = 4 * n + 2 * b
                    if c == BR0 + 1:
                        pe.wait_ge(mk_evac, 1)
                    if c == BR0 + 2:
                        pe.wait_ge(sb_exp, HEADS)
                    weights_T(c, aT_hi, aT_lo, 4 * b, 4, halves(o) + halves(o + 1), c + 1)

            for j in range(4):
                c = OUT0 + j
                pe.wait_ge(mix_lo, j + 1)
                if j == 0:
                    pe.wait_ge(mixed, 2)
                weights_move(c, mixT_hi, mixT_lo, 2 * j, 2, [[bank[0], bank[1]], [bank[2], bank[3]]], c + 1,
                             j == 0, j == 3, tiles=j == 3)

            pe.wait_ge(mix_lo, 4)
            weights_T(MK[1], mT_hi, mT_lo, 0, KT, halves(4), MK[1] + 1)
            transpose_stream(X1, res, x1_ready)
            mv_out = [[bank[b]] for b in MV_BANKS]
            weights_move(MV[0], mT_hi, mT_lo, 0, 4, mv_out, MV[0] + 1, True, False)

            pe.wait_ge(lo_done[X1], KT)
            pe.wait_ge(mk_evac, 2)

            def cross_scores(p):
                pe.wait_ge(xq_evac, p + 1)
                for h in (2 * p, 2 * p + 1):
                    for t in range(TOK):
                        last = mm(bank[X_S[h]][:, SEQ * t:SEQ * t + SEQ], xqT[:, h, t * P:(t + 1) * P], mkT[:, h, :],
                                  start=True, stop=True)
                    last.then_inc(x_s, 1)

            weights_T(XQ0, hT_hi, hT_lo, 0, KT, halves(7), XQ0 + 1)
            weights_T(XQ0 + 1, hT_hi, hT_lo, 0, KT, halves(4), XQ0 + 2, None, lambda: cross_scores(0))
            weights_move(MV[1], mT_hi, mT_lo, 4, 4, mv_out, MV[1] + 1, False, True,
                         between=lambda: cross_scores(1))
            for h in range(XH):
                pe.wait_ge(x_normed, h + 1)
                b_ = bank[X_PT[h]]
                for kt in range(2):
                    for t in range(TOK):
                        last = tr(b_[:, SEQ * kt + P * t:SEQ * kt + P * t + P],
                                  x_p[:, h, SEQ * t + P * kt:SEQ * t + P * kt + P], ident[:, :])
                last.then_inc(x_t, 1)
            pe.wait_ge(mv_evac, TOK)
            for h in range(XH):
                pe.wait_ge(x_pt, h + 1)
                for kt in range(2):
                    last = mm(bank[h // 2][:, SEQ * (h % 2):SEQ * (h % 2) + SEQ], mv_tok[:, kt, XDH * h:XDH * h + XDH],
                              x_pT[:, h, SEQ * kt:SEQ * kt + SEQ], start=kt == 0, stop=kt == 1)
                last.then_inc(x_av, 1)

            acc = [[bank[2], bank[3]], [bank[5], bank[6]]]
            for j in range(2):
                pe.wait_ge(xo_lo, j + 1)
                weights_move(XO0 + j, aT_hi, aT_lo, 2 * j, 2, acc, XO0 + j + 1, j == 0, j == 1, tiles=j == 1)
            transpose_stream(X2, res, x2_ready)

            def up(u, i=0, kt_wait=None):
                if u >= 2:
                    pe.wait_ge(u_relu, BODY // 2 * i + (u - 1))
                c = UP0 + max(2 * u - 1, 0)
                weights_T(c, hT_hi, hT_lo, 0, KT, halves(u % 2), BODY * i + (c + 1), kt_wait)

            def down(u, i=0, start=False, stop=False):
                pe.wait_ge(u_lo, BODY // 2 * i + (u + 1))
                c = min(UP0 + 2 * u + 2, LAST)
                weights_move(c, aT_hi, aT_lo, 4 + 2 * (u % 2), 2, acc, BODY * i + (c + 1), start, stop, tiles=stop)

            up(0, kt_wait=lambda k: pe.wait_ge(lo_done[X2], k + 1))
            up(1)
            down(0, start=True)
            first = 2 + PEEL // 2
            for u in range(2, first):
                up(u)
                down(u - 1)
            with pe.Fori(0, ITERS) as i:
                for u in range(first, first + BODY // 2):
                    up(u, i)
                    down(u - 1, i)
            down(PAIRS - 1, stop=True)


def kernel(**inputs):
    import numpy as np
    import concourse.bacc as bacc
    from concourse.bass_utils import run_bass_kernel_spmd

    def transposed(a):
        return a[0].T.reshape(-1, P, a.shape[1]).transpose(1, 0, 2)

    ff, width, xw = inputs["w_up"].shape[2], inputs["w_br_moba"].shape[1], inputs["w_xq"].shape[2]
    chunks, _ = weight_chunks(width, xw, inputs["x"].shape[2], ff)
    weights = np.stack([inputs[w][0, k0 * P:(k0 + nk) * P, c0:c0 + nc_].reshape(nk, P, nc_).transpose(1, 0, 2)
                        .reshape(P, nk * nc_) for w, k0, nk, c0, nc_ in chunks])
    gains = np.concatenate([inputs[g][0].reshape(-1, P).T for g in ("g_mix", "g_cross", "g_mem", "g_mlp")], axis=1)
    laid_out = {"x": inputs["x"], "xT": transposed(inputs["x"]), "mem": inputs["mem"],
                "memT": transposed(inputs["mem"]), "gains": gains, "g_final": inputs["g_final"], "weights": weights}

    nc = bacc.Bacc("TRN2", target_bir_lowering=False, num_devices=1)
    arrays, args = {}, []
    for name, a in laid_out.items():
        a = np.ascontiguousarray(a)
        arrays[f"in_{name}_dram"] = a
        args.append(nc.dram_tensor(f"in_{name}_dram", a.shape, mybir.dt.from_np(a.dtype), kind="ExternalInput").ap())
    shape = inputs["x"].shape
    out = nc.dram_tensor("out_dram", shape, mybir.dt.float32, kind="ExternalOutput").ap()
    hybrid_layer(nc, *args, ff, out)
    return run_bass_kernel_spmd(nc, [arrays], core_ids=[0]).results[0]["out_dram"]
```
